# Optimizing a Trainium2 kernel written in Bass

```python
import jax
import jax.numpy as jnp
from jax import lax
import numpy as np

D_MODEL = 1024
BATCH = 1
SEQ = 1024
DEPTH = 1

NORM_EPS = 1e-6
RWKV_HEAD = 64
RWKV_HEADS = 8
RWKV_DIM = RWKV_HEADS * RWKV_HEAD
DECAY_LORA = 64
ICLR_LORA = 64
GATE_LORA = 160
GN_EPS = 64e-5
MLA_HEADS = 8
Q_LORA = 256
KV_LORA = 128
NOPE_DIM = 64
ROPE_DIM = 32
V_DIM = 64
ROPE_THETA = 10000.0
Q_BLOCK = 128
D_FF = 4 * D_MODEL

RWKV_SIZES = (RWKV_DIM, RWKV_DIM, RWKV_DIM, DECAY_LORA, ICLR_LORA, GATE_LORA)
RWKV_COLS = 3 * RWKV_DIM + DECAY_LORA + ICLR_LORA + GATE_LORA
IN_SIZES = (RWKV_COLS, Q_LORA, KV_LORA, ROPE_DIM, D_MODEL, D_MODEL)
IN_COLS = RWKV_COLS + Q_LORA + KV_LORA + ROPE_DIM + 2 * D_MODEL

kernel_name = 'hybrid_rwkv7_mla_gated_block'

def _split(z, sizes):
    idx = []
    acc = 0
    for s in sizes[:-1]:
        acc += s
        idx.append(acc)
    return jnp.split(z, idx, axis=-1)

def rms_norm(x, g, eps=NORM_EPS):
    xf = x.astype(jnp.float32)
    y = xf * lax.rsqrt(jnp.mean(xf * xf, axis=-1, keepdims=True) + eps)
    return (y * g.astype(jnp.float32)).astype(x.dtype)

def token_shift(z, mu):
    prev = jnp.pad(z, ((0, 0), (1, 0), (0, 0)))[:, :-1]
    return z + (prev - z) * mu

def apply_rope(x, cos, sin):
    half = x.shape[-1] // 2
    x1, x2 = x[..., :half], x[..., half:]
    return jnp.concatenate([x1 * cos - x2 * sin, x2 * cos + x1 * sin], axis=-1)

def rwkv7_scan(r, decay, k, v, a, b):
    def step(state, inp):
        r_t, w_t, k_t, v_t, a_t, b_t = inp
        sa = jnp.einsum('bhvk,bhk->bhv', state, a_t)
        state = (state * w_t[:, :, None, :] + sa[..., None] * b_t[:, :, None, :]
                 + v_t[..., None] * k_t[:, :, None, :])
        y_t = jnp.einsum('bhvk,bhk->bhv', state, r_t)
        return state, y_t
    B, S, H, N = r.shape
    xs = tuple(jnp.moveaxis(t, 1, 0) for t in (r, decay, k, v, a, b))
    s0 = jnp.zeros((B, H, N, N), jnp.float32)
    _, ys = lax.scan(step, s0, xs)
    return jnp.moveaxis(ys, 0, 1)

def rwkv7_branch(zr, zk, zv, zw, za, zg, w0, w_up, a0, a_up, g_up, k_k, k_a, r_k,
                 ln_w, ln_b, w_o):
    f32 = jnp.float32
    B, S, _ = zr.shape
    heads = lambda t: t.reshape(B, S, RWKV_HEADS, RWKV_HEAD)
    w_pre = (w0 + jnp.tanh(zw) @ w_up).astype(f32)
    decay = jnp.exp(-jnp.exp(-jax.nn.softplus(-w_pre) - 0.5))
    a = jax.nn.sigmoid((a0 + za @ a_up).astype(f32))
    g = jax.nn.sigmoid(zg) @ g_up
    kk = heads((zk * k_k).astype(f32))
    kk = kk / jnp.maximum(jnp.linalg.norm(kk, axis=-1, keepdims=True), 1e-12)
    k = zk.astype(f32) * (1.0 + (a - 1.0) * k_a.astype(f32))
    r = heads(zr.astype(f32))
    k = heads(k)
    v = heads(zv.astype(f32))
    a = heads(a)
    y = rwkv7_scan(r, heads(decay), k, v, -kk, kk * a)
    mean = jnp.mean(y, axis=-1, keepdims=True)
    var = jnp.mean(jnp.square(y - mean), axis=-1, keepdims=True)
    y = (y - mean) * lax.rsqrt(var + GN_EPS)
    y = y.reshape(B, S, RWKV_DIM) * ln_w.astype(f32) + ln_b.astype(f32)
    bonus = jnp.sum(r * k * r_k.astype(f32), axis=-1, keepdims=True) * v
    y = (y + bonus.reshape(B, S, RWKV_DIM)) * g.astype(f32)
    return y.astype(zr.dtype) @ w_o

def mla_branch(c_q, c_kv, k_rope, cos, sin, q_norm, w_uq, kv_norm, w_ukv, w_o):
    B, S, _ = c_q.shape
    q = (rms_norm(c_q, q_norm) @ w_uq).reshape(B, S, MLA_HEADS, NOPE_DIM + ROPE_DIM)
    q_nope = q[..., :NOPE_DIM]
    q_rope = apply_rope(q[..., NOPE_DIM:], cos[:, :, None, :], sin[:, :, None, :])
    kv = (rms_norm(c_kv, kv_norm) @ w_ukv).reshape(B, S, MLA_HEADS, NOPE_DIM + V_DIM)
    k_nope = kv[..., :NOPE_DIM]
    v = kv[..., NOPE_DIM:]
    k_rope = apply_rope(k_rope, cos, sin)
    nb = S // Q_BLOCK
    qn_blocks = q_nope.reshape(B, nb, Q_BLOCK, MLA_HEADS, NOPE_DIM).transpose(1, 0, 3, 2, 4)
    qr_blocks = q_rope.reshape(B, nb, Q_BLOCK, MLA_HEADS, ROPE_DIM).transpose(1, 0, 3, 2, 4)
    kn = k_nope.transpose(0, 2, 1, 3)
    vh = v.transpose(0, 2, 1, 3)
    key_idx = jnp.arange(S)
    scale = (NOPE_DIM + ROPE_DIM) ** -0.5
    neg = jnp.finfo(jnp.float32).min

    def attend(args):
        qn_b, qr_b, blk = args
        s = (jnp.einsum('bhqd,bhkd->bhqk', qn_b, kn)
             + jnp.einsum('bhqr,bkr->bhqk', qr_b, k_rope))
        s = s.astype(jnp.float32) * scale
        q_idx = blk * Q_BLOCK + jnp.arange(Q_BLOCK)
        s = jnp.where(key_idx[None, :] <= q_idx[:, None], s, neg)
        p = jax.nn.softmax(s, axis=-1)
        return jnp.einsum('bhqk,bhkd->bhqd', p.astype(vh.dtype), vh)

    o = lax.map(attend, (qn_blocks, qr_blocks, jnp.arange(nb)))
    o = o.transpose(1, 0, 3, 2, 4).reshape(B, S, MLA_HEADS * V_DIM)
    return o @ w_o

def setup_inputs(seed: int = 0) -> dict:
    key = jax.random.key(seed)
    ks = jax.random.split(key, 32)
    f32 = jnp.float32
    L = DEPTH

    def nrm(k, shape, scale):
        return jax.random.normal(k, shape, f32) * scale

    def gain(k, shape):
        return 1.0 + 0.05 * jax.random.normal(k, shape, f32)

    return {
        'x': jax.random.normal(ks[0], (BATCH, SEQ, D_MODEL), f32),
        'positions': jnp.broadcast_to(jnp.arange(SEQ, dtype=jnp.int32)[None, :], (BATCH, SEQ)),
        'norm_mix': gain(ks[1], (L, D_MODEL)),
        'w_in': nrm(ks[2], (L, D_MODEL, IN_COLS), D_MODEL ** -0.5),
        'mu_shift': jax.random.uniform(ks[3], (L, RWKV_COLS), f32, 0.0, 1.0),
        'w0': jax.random.uniform(ks[4], (L, RWKV_DIM), f32, -6.0, 1.0),
        'w_up': nrm(ks[5], (L, DECAY_LORA, RWKV_DIM), 0.5 * DECAY_LORA ** -0.5),
        'a0': nrm(ks[6], (L, RWKV_DIM), 0.5),
        'a_up': nrm(ks[7], (L, ICLR_LORA, RWKV_DIM), 0.5 * ICLR_LORA ** -0.5),
        'g_up': nrm(ks[8], (L, GATE_LORA, RWKV_DIM), GATE_LORA ** -0.5),
        'k_k': 0.85 + 0.05 * jax.random.normal(ks[9], (L, RWKV_DIM), f32),
        'k_a': gain(ks[10], (L, RWKV_DIM)),
        'r_k': nrm(ks[11], (L, RWKV_HEADS, RWKV_HEAD), 0.1),
        'ln_w': gain(ks[12], (L, RWKV_DIM)),
        'ln_b': nrm(ks[13], (L, RWKV_DIM), 0.02),
        'w_o_rwkv': nrm(ks[14], (L, RWKV_DIM, D_MODEL), RWKV_DIM ** -0.5),
        'q_norm': gain(ks[15], (L, Q_LORA)),
        'w_uq': nrm(ks[16], (L, Q_LORA, MLA_HEADS * (NOPE_DIM + ROPE_DIM)), Q_LORA ** -0.5),
        'kv_norm': gain(ks[17], (L, KV_LORA)),
        'w_ukv': nrm(ks[18], (L, KV_LORA, MLA_HEADS * (NOPE_DIM + V_DIM)), KV_LORA ** -0.5),
        'w_o_mla': nrm(ks[19], (L, MLA_HEADS * V_DIM, D_MODEL), (MLA_HEADS * V_DIM) ** -0.5),
        'w_out': nrm(ks[20], (L, D_MODEL, D_MODEL), D_MODEL ** -0.5),
        'norm_ffn': gain(ks[21], (L, D_MODEL)),
        'w_ff_up': nrm(ks[22], (L, D_MODEL, D_FF), D_MODEL ** -0.5),
        'w_ff_down': nrm(ks[23], (L, D_FF, D_MODEL), D_FF ** -0.5),
        'norm_final': gain(ks[24], (D_MODEL,)),
    }

def reference(x, positions, norm_mix, w_in, mu_shift, w0, w_up, a0, a_up, g_up, k_k, k_a,
              r_k, ln_w, ln_b, w_o_rwkv, q_norm, w_uq, kv_norm, w_ukv, w_o_mla, w_out,
              norm_ffn, w_ff_up, w_ff_down, norm_final):
    half = ROPE_DIM // 2
    inv_freq = 1.0 / (ROPE_THETA ** (jnp.arange(half, dtype=jnp.float32) * (2.0 / ROPE_DIM)))
    ang = positions.astype(jnp.float32)[..., None] * inv_freq
    cos = jnp.cos(ang).astype(x.dtype)
    sin = jnp.sin(ang).astype(x.dtype)
    h = x
    for l in range(DEPTH):
        u = rms_norm(h, norm_mix[l])
        proj = u @ w_in[l]
        z_rwkv, c_q, c_kv, k_rope, gate_a, gate_b = _split(proj, IN_SIZES)
        z_rwkv = token_shift(z_rwkv, mu_shift[l])
        zr, zk, zv, zw, za, zg = _split(z_rwkv, RWKV_SIZES)
        y_a = rwkv7_branch(zr, zk, zv, zw, za, zg, w0[l], w_up[l], a0[l], a_up[l], g_up[l],
                           k_k[l], k_a[l], r_k[l], ln_w[l], ln_b[l], w_o_rwkv[l])
        y_b = mla_branch(c_q, c_kv, k_rope, cos, sin, q_norm[l], w_uq[l], kv_norm[l],
                         w_ukv[l], w_o_mla[l])
        merged = jax.nn.sigmoid(gate_a) * y_a + jax.nn.sigmoid(gate_b) * y_b
        h = h + merged @ w_out[l]
        f = rms_norm(h, norm_ffn[l]) @ w_ff_up[l]
        h = h + jnp.square(jax.nn.relu(f)) @ w_ff_down[l]
    return rms_norm(h, norm_final)


_drawn_inputs = setup_inputs


def setup_inputs(seed=0):
    import zlib

    import numpy as np

    out = dict(_drawn_inputs(seed))
    spreads = {}
    factors = {'w_up': 7.22,
     'k_k': 29.616,
     'k_a': 3.076,
     'ln_w': 17.054,
     'ln_b': 40.959,
     'q_norm': 8.0,
     'kv_norm': 8.0,
     'norm_ffn': 3.563,
     'r_k': 3.512}
    for name, (base, spread) in spreads.items():
        noise = np.random.default_rng([zlib.crc32(name.encode()), seed]).standard_normal(out[name].shape)
        drawn = base * np.exp(spread * noise) if base else spread * noise
        out[name] = jnp.asarray(drawn.astype(out[name].dtype))
    for name, factor in factors.items():
        out[name] = (out[name] * factor).astype(out[name].dtype)
    return out
```

```python
import numpy as np
import concourse.bass as bass
from concourse import mybir
from contextlib import ExitStack

F32, F32R, I32 = mybir.dt.float32, mybir.dt.float32r, mybir.dt.int32
ALU = mybir.AluOpType
ACT = mybir.ActivationFunctionType
AXX = mybir.AxisListType.X

P = 128
T, D, FF = 1024, 1024, 4096
NT, KD, NF = T // P, D // P, FF // P
HALF = 512
NH = 8
RH = 64
RD = NH * RH
RC = RD // P
LORA_G = 160
RWKV_COLS = 3 * RD + 64 + 64 + LORA_G
NRC = -(-RWKV_COLS // P)
QL, KVL, ROPE, NOPE, VD = 256, 128, 32, 64, 64
CC = QL + KVL + ROPE
QH = NOPE + ROPE
GATE0 = RWKV_COLS + CC
CH = 64
NC = T // CH
BL = 32
NG = FF // (2 * P)
GC = 2 * D // P
G0 = NRC
DECAY = float(np.exp(-0.5))
NORM_EPS, GN_EPS = 1e-6, 64e-5
SM_SCALE = float(QH) ** -0.5
NEG = -3.0e38
KB = 256

VROWS = [("norm_mix", KD, P), ("norm_ffn", KD, P), ("mu", RWKV_COLS // P, P), ("mu_tail", 1, RWKV_COLS % P),
         ("w0", RC, P), ("a0", RC, P), ("k_k", RC, P), ("k_a", RC, P), ("r_k", RC, P),
         ("q_norm", QL // P, P), ("kv_norm", 1, P)]
VAT, _n = {}, 0
for _name, _rows, _w in VROWS:
    VAT[_name] = _n
    _n += _rows
NV = _n


INV_FREQ = (1.0 / (np.float32(10000.0) ** (np.arange(ROPE // 2, dtype=np.float32) * np.float32(2.0 / ROPE)))).astype(np.float32)
ROUND_MAGIC = 1.5 * 2.0 ** 23
TWO_PI = (6.28125, 0.0019350051879882812, 3.01991598e-07)


def halves(u):
    return 1 if u // NH < 4 else 2


groups = halves


def second_of(u):
    return max(0, u - 4 * NH)


def ex_of(u):
    return u + second_of(u)


pt_of = ex_of


class Chain:

    def __init__(self, sem):
        self.sem, self.base, self.n = sem, 0, 0

    def __call__(self, eng, ins):
        self.n += 1
        ins.then_inc(self.sem, 1)
        eng.wait_ge(self.sem, self.base + self.n)

    def enter(self, i, per):
        self.outer, self.per = self.base + self.n, per
        self.base, self.n = self.outer + i * per, 0

    def leave(self, trips):
        assert self.n == self.per, (self.n, self.per)
        self.base, self.n = self.outer + trips * self.per, 0


def program(nc, a, out):
    ctx = ExitStack()
    top = {}

    def place(at_kb, *tensors):
        with ExitStack() as here:
            if at_kb:
                here.enter_context(nc.sbuf_tensor(f"gap{len(top)}", [P, int(at_kb * KB)], F32))
            got = [here.enter_context(nc.sbuf_tensor(n, s, t)) for n, s, t in tensors]
        used = at_kb + sum(int(np.prod(s[1:])) for _, s, _ in tensors) / KB
        top[tensors[0][0]] = used
        assert used <= 207, (tensors[0][0], used)
        return got

    def sem(name):
        return ctx.enter_context(nc.semaphore(name))

    with ctx:
        (ident, vcol, vrow, bones, small, cneg, cmask, cosv, sinv, kr, rope_t,
         lam, sbon) = place(
            0, ("ident", [P, P], F32), ("vcol", [P, 64], F32), ("vrow", [P, P], F32), ("bones", [P, P], F32),
            ("small", [P, 256], F32), ("cneg", [P, P], F32), ("cmask", [P, 2, 256], F32),
            ("cosv", [P, NT, 16], F32), ("sinv", [P, NT, 16], F32),
            ("kr", [P, NT, ROPE], F32), ("rope_t", [P, 4, NH, 16], F32),
            ("lam", [P, RC, NC], F32), ("sbon", [P, NT, RC, 2], F32))
        assert top["ident"] <= 11
        uT = place(11, ("uT_hi", [P, KD, T], F32R), ("uT_lo", [P, KD, T], F32R))
        xt, xjunk = place(75, ("xt", [P, NT, D], F32), ("xjunk", [P, D], F32))
        wc_raw, wc_hi, wc_lo, cnat = place(
            111, ("wc_raw", [P, KD, CC], F32), ("wc_hi", [P, KD, CC], F32R), ("wc_lo", [P, KD, CC], F32R),
            ("cnat", [P, NT, CC], F32))
        cT = place(163, ("cT_hi", [P, 3, T], F32R), ("cT_lo", [P, 3, T], F32R))
        uq_raw, ukv_raw = place(188, ("uq_raw", [P, 2, NH * QH], F32), ("ukv_raw", [P, NH * P], F32))
        invf, posr, posi, ang, ang_n = place(
            198, ("invf", [P, 16], F32), ("posr", [P, P], F32), ("posi", [P, P], I32),
            ("ang", [P, NT, 16], F32), ("ang_n", [P, NT, 16], F32))
        uq_hi, uq_lo, ukv_hi, ukv_lo = place(
            75, ("uq_hi", [P, 2, NH * QH], F32R), ("uq_lo", [P, 2, NH * QH], F32R),
            ("ukv_hi", [P, NH * P], F32R), ("ukv_lo", [P, NH * P], F32R))
        qT, kT, q_nat = place(95, ("qT", [P, NH, T], F32), ("kT", [P, NH, T], F32), ("q_nat", [P, NH, QH], F32))
        vm, k_nat = place(188, ("vm", [P, NT, NH * VD], F32), ("k_nat", [P, NH, QH], F32))
        pexp, pT, onat = place(75, ("pexp", [P, 2, T], F32), ("pT", [P, 2, NT, P], F32), ("onat", [P, 2, RD], F32))
        oT, = place(172, ("oT", [P, 4, T], F32))
        w_raw, w_hi, w_lo = place(75, ("w_raw", [P, 2, KD, P], F32), ("w_hi", [P, 2, KD, P], F32R), ("w_lo", [P, 2, KD, P], F32R))
        zbuf, zdif = place(99, ("zbuf", [P, 2, T + 1], F32), ("zdif", [P, T], F32))
        z, = place(112, ("z", [P, NRC, T], F32))
        iclr, kk, rn, cum = place(144, ("iclr", [P, T], F32), ("kk", [P, T], F32), ("rn", [P, T], F32), ("cum", [P, T], F32))
        einv, = place(164, ("einv", [P, T], F32))
        gbuf, edec = place(99, ("gbuf", [P, 2, T], F32), ("edec", [P, NC, CH + 1], F32))
        bT, aT, wau = place(172, ("bT", [P, RC, T], F32), ("aT", [P, RC, T], F32), ("wau", [P, P], F32))
        zz, lc, lp, xs, xprod = place(
            11, ("zz", [P, NT * NH, P], F32), ("lc", [P, NT, NH, BL], F32), ("lp", [P, 2, BL, BL], F32),
            ("xs", [P, 2, BL, BL], F32), ("xprod", [P, 2, 256], F32))
        mq_even, y1, q2_even, taw, tat = place(
            43, ("mq_even", [P, 2, RC, 512], F32), ("y1", [P, 2, 256], F32), ("q2_even", [P, 256], F32),
            ("taw", [P, 2, RC, 256], F32), ("tat", [P, 2, RC, P], F32))
        nat, mq_odd = place(75, ("nat", [P, 2, RC, 4, P], F32), ("mq_odd", [P, 2, RC, 512], F32))
        mq = (mq_even, mq_odd)
        wv = (cosv[:].rearrange("p i j -> p (i j)"), sinv[:].rearrange("p i j -> p (i j)"))
        q2 = (q2_even[:], kr[:].rearrange("p i j -> p (i j)"))
        lnw, lnb, stmp = place(107, ("lnw", [P, RD], F32), ("lnb", [P, RD], F32), ("stmp", [P, RC, RH], F32))
        vT, usb, state = place(
            144, ("vT", [P, RC, T], F32), ("usb", [P, 2, RD], F32), ("state", [P, 4, RC, P], F32))
        yc, ysq = place(204, ("yc", [P, RD], F32), ("ysq", [P, 256], F32))
        yin = place(11, ("yin_hi", [P, RC, T], F32R), ("yin_lo", [P, RC, T], F32R))
        oin = place(43, ("oin_hi", [P, RC, T], F32R), ("oin_lo", [P, RC, T], F32R))
        gT, oraw = place(75, ("gT", [P, RC, T], F32), ("oraw", [P, RC, T], F32))
        wo_raw, wo_hi, wo_lo = place(107, ("wo_raw", [P, 2, 2, RC, P], F32), ("wo_hi", [P, 2, 2, RC, P], F32R),
                                     ("wo_lo", [P, 2, 2, RC, P], F32R))
        mg = place(75, ("mg_hi", [P, KD, T], F32R)) + place(131, ("mg_lo", [P, KD, T], F32R))
        sgate, mtmp = place(163, ("sgate", [P, 2, 2, T], F32), ("mtmp", [P, 2, HALF], F32))
        gup, sg2 = place(183, ("gup", [P, 2, RD], F32), ("sg2", [P, 2, T], F32))
        wout = place(11, ("wout_hi", [P, KD, D], F32R), ("wout_lo", [P, KD, D], F32R))
        wout_raw, = place(107, ("wout_raw", [P, 6, D], F32))
        wout_sem = [(4, 32), (5, 32)] + [(i, 16 + 16 * KD + 16) for i in range(4)] + [(4, 48), (5, 48)]
        hacc, = place(163, ("hacc", [P, NT, D], F32))
        hjunk, hjunk2 = place(203, ("hjunk", [P, D], F32)) + place(135, ("hjunk2", [P, D], F32))
        hn, = place(75, ("hn", [P, NT, D], F32))
        hT = place(11, ("hT_hi", [P, KD, T], F32R), ("hT_lo", [P, KD, T], F32R))
        f_hi, f_lo = place(75, ("f_hi", [P, 2, 2, T], F32R), ("f_lo", [P, 2, 2, T], F32R))
        up_raw, up_hi, up_lo = place(107, ("up_raw", [P, 2, KD, P], F32), ("up_hi", [P, 2, KD, P], F32R), ("up_lo", [P, 2, KD, P], F32R))
        dn_hi, dn_lo = place(131, ("dn_hi", [P, 2, 2, D], F32R), ("dn_lo", [P, 2, 2, D], F32R))
        dn_raw, frelu = place(195, ("dn_raw", [P, 2, D], F32), ("frelu", [P, T], F32))
        nfin, = place(131, ("nfin", [P, D], F32))
        l_dram = nc.dram_tensor("l_spill", [NT * NH, P, BL], F32)
        x_dram = nc.dram_tensor("x_spill", [NT * NH, 2, 2, BL, BL], F32)
        v_dram = nc.dram_tensor("v_spill", [P, RC, T], F32)
        g_dram = nc.dram_tensor("g_spill", [P, 2, T], F32)
        o_dram = nc.dram_tensor("o_spill", [P, 4, T], F32)
        gate_dram = nc.dram_tensor("gate_spill", [2 * KD, P, T], F32)
        ps = [ctx.enter_context(nc.psum_tensor(f"bank{i}", [P, 512], F32)) for i in range(8)]

        s_x = [sem(f"tile_or_slot_loaded{i}") for i in range(NT)]
        s_vec = sem("vectors_loaded")
        s_const = sem("constants_made")
        s_vcol = sem("vcol_ready")
        s_vt = sem("vcol_transposed")
        s_ss = sem("row_squares")
        s_rt = sem("row_roots")
        s_xn = sem("x_normed")
        s_tr = sem("normed_rows_transposed")
        s_hi = sem("uT_hi_done")
        s_lo = sem("uT_lo_done")
        s_wc = sem("wc_loaded")
        s_wch = sem("wc_hi_done")
        s_wcl = sem("wc_lo_done")
        s_cp = sem("c_projected")
        s_ce = sem("c_evacuated")
        s_pos = sem("positions_loaded")
        s_posf = sem("positions_float")
        s_post = sem("positions_transposed")
        s_sin = sem("angles_and_sines")
        s_css = sem("c_squares")
        s_crt = sem("c_roots")
        s_cn = sem("c_normed")
        s_ct = sem("c_transposed")
        s_cth = sem("cT_hi_done")
        s_ctl = sem("cT_lo_done")
        s_u = sem("up_weights_loaded")
        s_uh = sem("up_hi_done")
        s_ul = sem("up_lo_done")
        s_kr = sem("k_rope_rotated")
        s_qp = sem("qkv_projected")
        s_qe = sem("qkv_evacuated")
        s_ro = sem("qk_rotated")
        s_qt = sem("qk_transposed")
        s_qte = sem("qkT_evacuated")
        s_sc = sem("scores_done")
        s_mx = sem("negated_max_done")
        s_ex = sem("exp_done")
        s_pt = sem("probs_transposed")
        s_pe0 = sem("pT_first_evacuated")
        s_pe1 = sem("pT_second_evacuated")
        s_pv = sem("pv_done")
        s_on = sem("o_normed")
        s_ot = sem("o_transposed")
        s_ote = sem("oT_evacuated")
        s_cst2 = sem("masks_made")
        s_w = [sem(f"w_slot{b}_loaded") for b in range(2)]
        s_wh = sem("w_hi_done")
        s_wl = sem("w_lo_done")
        s_pj = sem("chunk_half_projected")
        s_ze = sem("chunk_half_evacuated")
        s_z0 = sem("zbuf_zeroed")
        s_sh = sem("tokens_shifted")
        s_spo = sem("o_spilled")
        s_spv = sem("v_spilled")
        s_spg = sem("g_spilled")
        s_zs = sem("tanh_and_g_sigmoid")
        s_gs = [sem(f"gates_slot{b}_stored") for b in range(2)]
        s_bias = sem("chunk_biases_placed")
        s_wau = sem("wau_loaded")
        s_pre = sem("w_and_a_projected")
        s_sg = sem("decay_and_iclr_sigmoids")
        s_cum = sem("decay_summed")
        s_e = sem("decay_exps")
        s_sq = sem("kk_squared")
        s_sq2 = sem("kk_square_summed")
        s_rc = sem("kk_norm_clamped")
        s_rr = sem("kk_norm_root")
        s_rk = sem("rk_products")
        s_bs = sem("bonus_summed")
        s_ew = sem("rwkv_chunk_ready")
        s_bo = sem("bones_made")
        s_lm = sem("L_products")
        s_lea = sem("L_evacuated_act")
        s_led = sem("L_evacuated_dve")
        s_ls = sem("L_stored")
        s_lp = sem("L_by_problem")
        s_x0 = sem("inverse_identity")
        s_xd = sem("inverse_done")
        s_xst = sem("inverse_stored")
        s_zz = sem("inverse_loaded")
        s_z0z = sem("zz_zeroed")
        s_v = sem("v_reloaded")
        s_ln = sem("ln_loaded")
        s_msk = sem("chunk_masks")
        s_tn = sem("naturals_transposed")
        s_nat = sem("naturals_evacuated")
        s_pr = [sem(f"products_head{h}") for h in range(2)]
        s_m = [sem(f"products_masked_head{h}") for h in range(2)]
        s_wm = sem("mv_product")
        s_we = sem("mv_evacuated")
        s_y1m = sem("block_solve_product")
        s_y1 = sem("block_solve_evacuated")
        s_q2m = sem("offblock_product")
        s_q2 = sem("offblock_evacuated")
        s_y2m = sem("correction_product")
        s_y2 = sem("solved")
        s_tm = sem("ta_transposed")
        s_tat = sem("ta_evacuated")
        s_um = sem("u_product")
        s_us = sem("u_ready")
        s_sm = sem("state_product")
        s_st = sem("state_ready")
        s_ym = sem("y_product")
        s_yc = sem("y_centered")
        s_ysq = sem("y_squared")
        s_yv = sem("y_variance")
        s_ysr = sem("y_squares_summed")
        s_yr = sem("y_root")
        s_yn = sem("y_normed")
        s_bv = sem("bonus_made")
        s_pn = sem("y_with_bonus")
        s_ytm = sem("y_transposed")
        s_yt = sem("yT_evacuated")
        s_gup = sem("gup_loaded")
        s_gm = sem("g_product")
        s_ge = sem("g_evacuated")
        s_or = sem("o_reloaded")
        s_yg = sem("yg_product")
        s_po = sem("branches_projected")
        s_mga = sem("branch_halves_read")
        s_mt = sem("merged_sum")
        s_mgh = sem("merged_hi_done")
        s_mgl = sem("merged_lo_done")
        s_hx = sem("x_reloaded")
        s_hm = sem("h_product")
        s_h = sem("h_added")
        s_dn = sem("dn_loaded")
        s_f = sem("f_product")
        s_fr = sem("f_relu")
        s_fe = sem("f_squared")
        s_fh = sem("f_hi_done")
        s_fl = sem("f_lo_done")
        s_dm = sem("down_product")
        s_da = sem("down_added")
        s_nf = sem("norm_final_loaded")
        s_fin = sem("rows_finished")
        s_out = sem("out_stored")
        dch, ach, pch = Chain(sem("dve_chain")), Chain(sem("act_chain")), Chain(sem("pool_chain"))

        x_d = a["x"][0].rearrange("(i p) d -> i p d", p=P)
        win = a["w_in"][0].rearrange("(k p) n -> p k n", p=P)

        with nc.Block() as block:

            @block.sync
            def _(sp):
                for i in range(NT):
                    sp.dma_start(xt[:, i, :], x_d[i]).then_inc(s_x[i], 16)
                sp.dma_start(wc_raw[:], win[:, :, RWKV_COLS:RWKV_COLS + CC]).then_inc(s_wc, 16)
                sp.dma_start(posi[0:NT, :], a["positions"][0].rearrange("(i p) -> i p", p=P)).then_inc(s_pos, 16)
                sp.dma_start(uq_raw[:], a["w_uq"][0].rearrange("(k p) n -> p k n", p=P)).then_inc(s_u, 16)
                sp.dma_start(ukv_raw[:], a["w_ukv"][0]).then_inc(s_u, 16)

                def load_w(n, slot, col):
                    sp.dma_start(w_raw[:, slot], win[:, :, bass.ds(col, P)]).then_inc(s_w[slot], 16)

                sp.wait_ge(s_ote, NT)
                sp.dma_start(o_dram[:], oT[:]).then_inc(s_spo, 16)
                sp.wait_ge(s_pv, NT * NH)
                for n in range(2):
                    load_w(n, n, n * P)
                with sp.Fori(1, NRC // 2) as j:
                    for b in range(2):
                        sp.wait_ge(s_wl, 2 * j + (b - 1))
                        load_w(2 * j + b, b, j * (2 * P) + b * P)
                sp.wait_ge(s_wl, NRC - 2)
                load_w(NRC - 1, 0, (NRC - 1) * P)
                sp.wait_ge(s_sh, 3 * RC)
                sp.dma_start(v_dram[:], z[:, 2 * RC:3 * RC, :]).then_inc(s_spv, 16)
                with sp.Fori(0, GC // 4) as c:
                    for q in range(4):
                        sp.wait_ge(s_wl, 4 * c + (G0 + q - 1))
                        load_w(G0 + q, (G0 + q) % 2, c * (4 * P) + (GATE0 + q * P))
                sp.wait_ge(s_ew, RC)
                sp.dma_start(vT[:], v_dram[:]).then_inc(s_v, 16)
                sp.dma_start(lnw[:], a["ln_w"][0:1, :].partition_broadcast(P)).then_inc(s_ln, 16)
                sp.dma_start(lnb[:], a["ln_b"][0:1, :].partition_broadcast(P)).then_inc(s_ln, 16)
                sp.wait_ge(s_lea, 2 * NT)
                sp.wait_ge(s_led, 2 * NT)
                sp.dma_start(l_dram[:].rearrange("n p s -> p n s"), lc[:].rearrange("p i h s -> p (i h) s")).then_inc(s_ls, 16)
                sp.wait_ge(s_ls, 16)
                sp.dma_start(lp[:].rearrange("p b t s -> p (b t s)"),
                             l_dram[:].rearrange("n (c r) s -> (n c) (r s)", c=2)).then_inc(s_lp, 16)
                sp.wait_ge(s_xd, 1)
                sp.dma_start(x_dram[:].rearrange("n c b s t -> (n c) (b s t)"), xs[:].rearrange("p b s t -> p (b s t)")).then_inc(s_xst, 16)
                sp.wait_ge(s_xst, 16)
                sp.wait_ge(s_z0z, 1)
                for r in range(4):
                    sp.dma_start(zz[32 * r:32 * r + 32, :, 32 * r:32 * r + 32],
                                 x_dram[:, r // 2, r % 2].rearrange("n s t -> s n t")).then_inc(s_zz, 16)

                wo_d = [a[n][0].rearrange("(k p) n -> p k n", p=P) for n in ("w_o_rwkv", "w_o_mla")]
                sp.wait_ge(s_tm, RC * NT)
                sp.dma_start(gup[:, 0, :], a["g_up"][0][0:P, :]).then_inc(s_gup, 16)
                sp.dma_start(gup[0:LORA_G - P, 1, :], a["g_up"][0][P:LORA_G, :]).then_inc(s_gup, 16)
                sp.dma_start(sg2[:], g_dram[:]).then_inc(s_gup, 16)
                sp.wait_ge(s_ym, NT)
                sp.dma_start(oraw[:], o_dram[:]).then_inc(s_or, 16)

                def load_wo(n, b):
                    for w in range(2):
                        sp.dma_start(wo_raw[:, b, w], wo_d[w][:, :, bass.ds(n * P, P)]).then_inc(s_x[0 + b], 16)

                def load_gates(n, b):
                    for w in range(2):
                        sp.dma_start(sgate[:, b, w, :], gate_dram[bass.ds(n + w * KD, 1)].rearrange("o p t -> p (o t)")).then_inc(s_x[2 + b], 16)

                sp.wait_ge(s_pn, NT)
                for b in range(2):
                    load_wo(b, b)
                    load_gates(b, b)
                with sp.Fori(1, KD // 2) as j:
                    for b in range(2):
                        sp.wait_ge(s_ul, 3 + 2 * j + (b - 1))
                        load_wo(2 * j + b, b)
                        sp.wait_ge(s_mt, 4 * j + (2 * b - 2))
                        load_gates(2 * j + b, b)
                sp.wait_ge(s_ul, 3 + KD)
                for k in range(KD):
                    if k == 2:
                        sp.wait_ge(s_po, 2 * KD)
                    if k == 4:
                        sp.wait_ge(s_mt, 2 * KD)
                    if k >= 6:
                        sp.wait_ge(s_wl, (G0 + GC) + k - 5)
                    sp.dma_start(wout_raw[:, k % 6, :], a["w_out"][0][k * P:(k + 1) * P, :]).then_inc(s_x[wout_sem[k][0]], 16)
                sp.wait_ge(s_mgl, 2 * KD)
                for i in range(NT):
                    sp.dma_start(hacc[:, i, :], x_d[i]).then_inc(s_hx, 16)
                up_d = a["w_ff_up"][0].rearrange("(k p) n -> p k n", p=P)
                dn_d = a["w_ff_down"][0].rearrange("(m p) n -> p m n", p=P)
                sp.wait_ge(s_wl, (G0 + GC) + KD)

                def load_up(n, b):
                    sp.dma_start(up_raw[:, b], up_d[:, :, bass.ds(n * P, P)]).then_inc(s_x[6 + b], 16)

                for b in range(2):
                    load_up(b, b)
                sp.dma_start(dn_raw[:], dn_d[:, 0:2, :]).then_inc(s_dn, 16)
                with sp.Fori(1, NG) as g:
                    for b in range(2):
                        sp.wait_ge(s_ul, (3 + KD) + 2 * g + (b - 1))
                        load_up(2 * g + b, b)
                    sp.wait_ge(s_ctl, (6 + RC) + g)
                    sp.dma_start(dn_raw[:], dn_d[:, bass.ds(2 * g, 2), :]).then_inc(s_dn, 16)
                sp.wait_ge(s_dm, 2 * NT * (NG - 1))
                sp.dma_start(nfin[:], a["norm_final"].rearrange("(o n) -> o n", o=1).partition_broadcast(P)).then_inc(s_nf, 16)
                out_d = out[0].rearrange("(i p) d -> i p d", p=P)
                for i in range(NT):
                    sp.wait_ge(s_fin, i + 1)
                    sp.dma_start(out_d[i], hacc[:, i, :]).then_inc(s_out, 16)
                sp.wait_ge(s_out, 16 * NT)

            @block.gpsimd
            def _(pool):
                pch(pool, nc.gpsimd.memset(ident[:], 0.0))
                nc.gpsimd.affine_select(out=ident[:], in_=ident[:], compare_op=ALU.not_equal, fill=1.0, base=0,
                                        pattern=[[-1, P]], channel_multiplier=1).then_inc(s_const, 1)

                for j in range(ROPE // 2):
                    ins = nc.gpsimd.memset(invf[:, j:j + 1], float(INV_FREQ[j]))
                ins.then_inc(s_const, 1)
                pch(pool, nc.gpsimd.memset(cneg[:], 0.0))
                nc.gpsimd.affine_select(out=cneg[:], in_=cneg[:], compare_op=ALU.is_ge, fill=NEG, base=0,
                                        pattern=[[-1, P]], channel_multiplier=1).then_inc(s_cst2, 1)

                def rotate(x1, x2, o1, o2, cos, sin, t):
                    nc.gpsimd.tensor_tensor(t[0], x1, cos, ALU.mult)
                    nc.gpsimd.tensor_tensor(t[1], x2, sin, ALU.mult)
                    nc.gpsimd.tensor_tensor(t[2], x2, cos, ALU.mult)
                    pch(pool, nc.gpsimd.tensor_tensor(t[3], x1, sin, ALU.mult))
                    nc.gpsimd.tensor_tensor(o1, t[0], t[1], ALU.subtract)
                    return nc.gpsimd.tensor_tensor(o2, t[2], t[3], ALU.add)

                pool.wait_ge(s_sin, 4)
                pool.wait_ge(s_ce, NT)
                flat = [rope_t[:, j, :, :] for j in range(4)]
                rotate(cnat[:, :, QL + KVL:QL + KVL + 16], cnat[:, :, QL + KVL + 16:CC], kr[:, :, 0:16], kr[:, :, 16:32],
                       cosv[:], sinv[:], flat).then_inc(s_kr, 1)
                pool.wait_ge(s_kr, 1)
                for i in range(NT):
                    pool.wait_ge(s_qe, 5 * (i + 1))
                    cb = cosv[:, i:i + 1, :].to_broadcast([P, NH, 16])
                    sb = sinv[:, i:i + 1, :].to_broadcast([P, NH, 16])
                    x1, x2 = q_nat[:, :, NOPE:NOPE + 16], q_nat[:, :, NOPE + 16:QH]
                    rotate(x1, x2, x1, x2, cb, sb, flat)
                    nc.gpsimd.tensor_scalar(k_nat[:, :, NOPE:QH], kr[:, i:i + 1, :].to_broadcast([P, NH, ROPE]),
                                            1.0, 0.0, ALU.mult, ALU.add).then_inc(s_ro, 1)

                nc.gpsimd.memset(bones[:], 0.0).then_inc(s_bo, 1)
                pool.wait_ge(s_bo, 1)
                nc.gpsimd.memset(bones[0:64, 0:64], 1.0).then_inc(s_bo, 1)
                pool.wait_ge(s_bo, 2)
                nc.gpsimd.memset(bones[64:128, 64:128], 1.0).then_inc(s_bo, 1)
                pool.wait_ge(s_bo, 3)
                pool.wait_ge(s_pv, NT * NH)
                nc.gpsimd.memset(zbuf[:, :, 0:1], 0.0).then_inc(s_z0, 1)
                pool.wait_ge(s_zs, 3)
                pool.dma_start(g_dram[:], z[:, NRC - 2:NRC, :]).then_inc(s_spg, 16)
                pool.wait_ge(s_sh, NRC)
                nc.gpsimd.memset(edec[:, :, 0:1], 1.0).then_inc(s_z0, 1)

                def load_wau(c):
                    pool.dma_start(wau[0:64, :], a["w_up"][0][:, bass.ds(c * P, P)]).then_inc(s_wau, 16)
                    pool.dma_start(wau[64:128, :], a["a_up"][0][:, bass.ds(c * P, P)]).then_inc(s_wau, 16)

                def store_gates(c):
                    for q in range(4):
                        slot = (G0 + q) % 2
                        pool.wait_ge(s_ze, 8 * c + (2 * (G0 + q) + 2))
                        pool.dma_start(gate_dram[bass.ds(4 * c + q, 1)].rearrange("o p t -> p (o t)"),
                                       gbuf[:, slot, :]).then_inc(s_gs[slot], 16)

                load_wau(0)
                store_gates(0)
                with pool.Fori(1, RC) as c:
                    pool.wait_ge(s_pre, 4 * c)
                    load_wau(c)
                    store_gates(c)

                pch(pool, nc.gpsimd.memset(cmask[:, 0, :], 0.0))
                pch(pool, nc.gpsimd.memset(cmask[:, 1, :], 1.0))
                for r in (0, 64):
                    pch(pool, nc.gpsimd.memset(cmask[r:r + 32, 0, r + 32:r + 64], 1.0))
                for w, base in ((0, -1), (1, 0)):
                    pch(pool, nc.gpsimd.affine_select(out=cmask[:, 1, w * P:(w + 1) * P], in_=cmask[:, 1, w * P:(w + 1) * P],
                                                      compare_op=ALU.is_ge, fill=0.0, base=base, pattern=[[1, P]],
                                                      channel_multiplier=-1))
                    pch(pool, nc.gpsimd.memset(cmask[0:64, 1, w * P + 64:(w + 1) * P], 0.0))
                nc.gpsimd.tensor_scalar(cmask[:, 0, P:2 * P], cmask[:, 1, P:2 * P], 1.0, 0.0, ALU.mult, ALU.add).then_inc(s_msk, 1)
                pool.wait_ge(s_pj, 2 * (G0 + GC))
                pool.wait_ge(s_msk, 1)
                pch(pool, nc.gpsimd.memset(xs[:], 0.0))
                nc.gpsimd.memset(xs[:].rearrange("p b s t -> p b (s t)")[:, :, 0:BL * BL:BL + 1], 1.0).then_inc(s_x0, 1)
                pool.wait_ge(s_x0, 1)
                nc.gpsimd.memset(zz[:], 0.0).then_inc(s_z0z, 1)
                pool.wait_ge(s_z0z, 1)
                pool.wait_ge(s_ew, RC)
                nc.gpsimd.memset(state[:], 0.0).then_inc(s_st, 1)
                pool.wait_ge(s_st, 1)
                pool.wait_ge(s_ln, 32)
                bonus = rope_t[:].rearrange("p a h j -> p (a h j)")
                for i in range(NT):
                    pool.wait_ge(s_nat, RC * (i + 1))
                    for c in range(RC):
                        for h in range(2):
                            v0 = slice(h * RH, (h + 1) * RH)
                            ins = nc.gpsimd.tensor_scalar(bonus[:, c * P + h * RH:c * P + (h + 1) * RH], nat[:, i % 2, c, 3, v0],
                                                          sbon[:, i, c, h:h + 1], 0.0, ALU.mult, ALU.add)
                    ins.then_inc(s_bv, 1)
                    pool.wait_ge(s_bv, i + 1)
                    pool.wait_ge(s_yn, i + 1)
                    pch(pool, nc.gpsimd.tensor_tensor(yc[:], yc[:], lnw[:], ALU.mult))
                    pch(pool, nc.gpsimd.tensor_tensor(yc[:], yc[:], lnb[:], ALU.add))
                    nc.gpsimd.tensor_tensor(yc[:], yc[:], bonus, ALU.add).then_inc(s_pn, 1)
                    pool.wait_ge(s_pn, i + 1)

            def evac_second(act, u):
                i = u // NH
                act.wait_ge(s_pt, pt_of(u) + 2)
                act.wait_ge(s_pv, u - 1)
                nc.scalar.activation(pT[:, u % 2, 4:i + 1, :], ps[7][:, 0:(i - 3) * P].rearrange("p (b q) -> p b q", q=P),
                                     ACT.Copy).then_inc(s_pe1, 1)

            @block.scalar
            def _(act):
                act.wait_ge(s_vec, 1)
                n = 0
                for name, rows, w in VROWS:
                    r0 = VAT[name]
                    if name == "mu":
                        src = a["mu_shift"][0, 0:rows * P].rearrange("(r w) -> r w", w=P)
                    elif name == "mu_tail":
                        src = a["mu_shift"][0:1, RWKV_COLS - w:RWKV_COLS]
                    elif name == "r_k":
                        src = a["r_k"][0].rearrange("(r q) k -> r (q k)", r=rows)
                    else:
                        src = a[name][0].rearrange("(r w) -> r w", w=P)
                    act.dma_start(vrow[r0:r0 + rows, 0:w], src).then_inc(s_vec, 16)
                for i in range(NT):
                    act.wait_ge(s_x[i], 16)
                    if i:
                        act.wait_ge(s_ss, i)
                    nc.scalar.activation(xjunk[:], xt[:, i, :], ACT.Square,
                                         accum_out=small[:, i:i + 1]).then_inc(s_ss, 1)
                act.wait_ge(s_rt, 1)
                nc.scalar.activation(small[:, 16:24], small[:, 8:16], ACT.Sqrt).then_inc(s_rt, 1)
                for n in range(2 * KD):
                    g, k = n // KD, n % KD
                    act.wait_ge(s_tr, n + 1)
                    if n == 0:
                        act.wait_ge(s_vcol, 1)
                    c = VAT["norm_mix"] + k
                    nc.scalar.activation(uT[0][:, k, g * HALF:(g + 1) * HALF], ps[n % 4][:], ACT.Copy,
                                         scale=vcol[:, c:c + 1]).then_inc(s_hi, 1)
                act.wait_ge(s_wc, 16)
                for k in range(KD):
                    nc.scalar.activation(wc_hi[:, k, :], wc_raw[:, k, :], ACT.Copy).then_inc(s_wch, 1)
                act.wait_ge(s_sin, 1)
                nc.scalar.activation(sinv[:], ang[:], ACT.Sin).then_inc(s_sin, 1)
                nc.scalar.activation(cosv[:], ang[:], ACT.Sin, scale=0.5).then_inc(s_sin, 1)
                for i in range(NT):
                    act.wait_ge(s_cp, i + 1)
                    nc.scalar.activation(cnat[:, i, :], ps[4 + i % 2][:, 0:CC], ACT.Copy).then_inc(s_ce, 1)
                for i in range(NT):
                    act.wait_ge(s_ce, i + 1)
                    if i:
                        act.wait_ge(s_css, 2 * i)
                    nc.scalar.activation(xjunk[:, 0:QL], cnat[:, i, 0:QL], ACT.Square,
                                         accum_out=small[:, 32 + i:33 + i]).then_inc(s_css, 1)
                    nc.scalar.activation(xjunk[:, QL:QL + KVL], cnat[:, i, QL:QL + KVL], ACT.Square,
                                         accum_out=small[:, 40 + i:41 + i]).then_inc(s_css, 1)
                act.wait_ge(s_crt, 1)
                nc.scalar.activation(small[:, 64:80], small[:, 48:64], ACT.Sqrt).then_inc(s_crt, 1)
                act.wait_ge(s_u, 32)
                act.wait_ge(s_lo, 2 * KD)
                for k in range(2):
                    nc.scalar.activation(uq_hi[:, k, :], uq_raw[:, k, :], ACT.Copy).then_inc(s_uh, 1)
                nc.scalar.activation(ukv_hi[:], ukv_raw[:], ACT.Copy).then_inc(s_uh, 1)
                for n in range(6):
                    c, g = n // 2, n % 2
                    act.wait_ge(s_ct, n + 1)
                    v = (VAT["q_norm"] + c) if c < 2 else VAT["kv_norm"]
                    nc.scalar.activation(cT[0][:, c, g * HALF:(g + 1) * HALF], ps[n % 4][:], ACT.Copy,
                                         scale=vcol[:, v:v + 1]).then_inc(s_cth, 1)

                def evac_qkv(i):
                    act.wait_ge(s_qp, 4 * i + 2)
                    if i:
                        act.wait_ge(s_qt, 4 * i)
                    for b in range(2):
                        nc.scalar.activation(q_nat[:, 4 * b:4 * b + 4, :],
                                             ps[b][:, 0:4 * QH].rearrange("p (h q) -> p h q", q=QH),
                                             ACT.Copy).then_inc(s_qe, 1)
                    for b in range(2):
                        act.wait_ge(s_qp, 4 * i + 3 + b)
                        kv = ps[2 + b][:].rearrange("p (h c) -> p h c", c=P)
                        nc.scalar.activation(k_nat[:, 4 * b:4 * b + 4, 0:NOPE], kv[:, :, 0:NOPE],
                                             ACT.Copy).then_inc(s_qe, 1)
                        last = nc.scalar.activation(vm[:, i, b * 256:(b + 1) * 256].rearrange("p (h c) -> p h c", c=VD),
                                                    kv[:, :, NOPE:P], ACT.Copy)
                    last.then_inc(s_qe, 1)

                act.wait_ge(s_kr, 1)
                for i in range(NT):
                    evac_qkv(i)
                    for b in range(2):
                        act.wait_ge(s_qt, 4 * i + 3 + b)
                        nc.scalar.activation(kT[0:QH, 4 * b:4 * b + 4, i * P:(i + 1) * P],
                                             ps[6 + b][0:QH, :].rearrange("p (h t) -> p h t", t=P),
                                             ACT.Copy).then_inc(s_qte, 1)

                for u in range(NT * NH):
                    i, h = u // NH, u % NH
                    n = (i + 1) * P
                    act.wait_ge(s_mx, u + 1)
                    if u >= 2:
                        act.wait_ge(s_pt, pt_of(u - 2) + groups(u - 2))
                    sc = small[:, 192 + u % 2:193 + u % 2]
                    b0 = 2 * (u % 2)
                    n0 = min(n, 512)
                    nc.scalar.activation(pexp[:, u % 2, 0:n0], ps[b0][:, 0:n0], ACT.Exp, bias=sc, scale=SM_SCALE,
                                         accum_out=small[:, 128 + 2 * h:129 + 2 * h] if i % 2 == 0 else small[:, 144 + 2 * h:145 + 2 * h]).then_inc(s_ex, 1)
                    if n > 512:
                        nc.scalar.activation(pexp[:, u % 2, 512:n], ps[b0 + 1][:, 0:n - 512], ACT.Exp, bias=sc, scale=SM_SCALE,
                                             accum_out=small[:, 129 + 2 * h:130 + 2 * h] if i % 2 == 0 else small[:, 145 + 2 * h:146 + 2 * h]).then_inc(s_ex, 1)
                    if u >= 1 and groups(u - 1) == 2:
                        evac_second(act, u - 1)
                evac_second(act, NT * NH - 1)

                def round_w(slot, loads, pe_done):
                    act.wait_ge(s_w[slot], loads)
                    if pe_done is not None:
                        act.wait_ge(s_pj, pe_done)
                    nc.scalar.activation(w_hi[:, slot], w_raw[:, slot], ACT.Copy).then_inc(s_wh, 1)

                def evac_z(slot, pj, sh):
                    for g in range(2):
                        act.wait_ge(s_pj, pj + (g + 1))
                        if sh is not None and g == 0:
                            act.wait_ge(s_sh, sh)
                        nc.scalar.activation(zbuf[:, slot, 1 + g * HALF:1 + (g + 1) * HALF], ps[2 * slot + g][:],
                                             ACT.Copy).then_inc(s_ze, 1)

                round_w(0, 16, None)
                round_w(1, 16, None)
                evac_z(0, 0, None)
                round_w(0, 32, 2)
                evac_z(1, 2, None)
                with act.Fori(1, NRC // 2) as j:
                    round_w(1, 16 * j + 16, 4 * j)
                    evac_z(0, 4 * j, 2 * j - 1)
                    round_w(0, 16 * j + 32, 4 * j + 2)
                    evac_z(1, 4 * j + 2, 2 * j)
                round_w(1, 16 * (G0 // 2 + 1), 2 * (G0 - 1))
                evac_z(0, 2 * (NRC - 1), NRC - 2)
                act.wait_ge(s_sh, NRC)
                nc.scalar.activation(z[0:64, 3 * RC, :], z[0:64, 3 * RC, :], ACT.Tanh).then_inc(s_zs, 1)
                nc.scalar.activation(z[:, NRC - 2, :], z[:, NRC - 2, :], ACT.Sigmoid).then_inc(s_zs, 1)
                nc.scalar.activation(z[:, NRC - 1, :], z[:, NRC - 1, :], ACT.Sigmoid).then_inc(s_zs, 1)

                act.wait_ge(s_spv, 16)
                act.wait_ge(s_spg, 16)
                def rwkv_chunk(c, last):
                    def gate(q):
                        n = G0 + q
                        slot = n % 2
                        for g in range(2):
                            act.wait_ge(s_pj, 8 * c + (2 * n + g + 1))
                            if g == 0 and not (isinstance(c, int) and c == 0 and q < 2):
                                act.wait_ge(s_gs[slot], 32 * c + 16 * (q // 2))
                            nc.scalar.activation(gbuf[:, slot, g * HALF:(g + 1) * HALF], ps[2 * slot + g][:],
                                                 ACT.Sigmoid).then_inc(s_ze, 1)

                    def round_gate(q):
                        n = G0 + q
                        round_w(n % 2, 32 * c + 16 * (n // 2 + 1), 8 * c + 2 * (n - 1))

                    for w, name in enumerate(("w0", "a0")):
                        ins = nc.scalar.activation(small[:, 250 + w:251 + w], vcol[:, bass.ds(c + VAT[name], 1)], ACT.Copy)
                    ins.then_inc(s_bias, 1)
                    round_gate(1)
                    gate(0)
                    act.wait_ge(s_bias, c + 1)
                    for g in range(2):
                        act.wait_ge(s_pre, 4 * c + (g + 1))
                        if g == 0 and not (isinstance(c, int) and c == 0):
                            act.wait_ge(s_ew, c)
                        nc.scalar.activation(kk[:, g * HALF:(g + 1) * HALF], ps[4 + g][:], ACT.Sigmoid,
                                             bias=small[:, 250:251]).then_inc(s_sg, 1)
                    for g in range(2):
                        act.wait_ge(s_pre, 4 * c + (g + 3))
                        nc.scalar.activation(iclr[:, g * HALF:(g + 1) * HALF], ps[6 + g][:], ACT.Sigmoid,
                                             bias=small[:, 251:252]).then_inc(s_sg, 1)
                    nc.scalar.activation(rn[:], z[:, bass.ds(c + RC, 1), :], ACT.Square,
                                         scale=vcol[:, bass.ds(c + VAT["k_k"], 1)]).then_inc(s_sq, 1)
                    round_gate(2)
                    gate(1)
                    act.wait_ge(s_cum, c + 1)
                    nc.scalar.activation(edec[:, :, 1:CH + 1], cum[:].rearrange("p (n t) -> p n t", t=CH), ACT.Exp,
                                         scale=-DECAY).then_inc(s_e, 1)
                    nc.scalar.activation(einv[:], cum[:], ACT.Exp, scale=DECAY).then_inc(s_e, 1)
                    nc.scalar.activation(lam[:, bass.ds(c, 1), :], cum[:].rearrange("p (n t) -> p t n", t=CH)[:, CH - 1, :],
                                         ACT.Exp, scale=-DECAY).then_inc(s_e, 1)
                    act.wait_ge(s_rc, 2 * c + 2)
                    nc.scalar.activation(rn[:], rn[:], ACT.Sqrt).then_inc(s_rr, 1)
                    round_gate(3)
                    gate(2)
                    if not last:
                        round_gate(4)
                    gate(3)

                rwkv_chunk(0, False)
                with act.Fori(1, RC - 1) as c:
                    rwkv_chunk(c, False)
                rwkv_chunk(RC - 1, True)

                for n in range(2 * NT):
                    act.wait_ge(s_lm, n + 1)
                    for r in (0, 32):
                        ins = nc.scalar.activation(lc[r:r + 32, n // 2, n % 2:NH:2, :],
                                                   ps[n % 2][r:r + 32, :].rearrange("p (h s) -> p h s", s=P)[:, :, r:r + 32],
                                                   ACT.Copy)
                    ins.then_inc(s_lea, 1)

                def nat_evac(s):
                    i, c = divmod(s, RC)
                    act.wait_ge(s_tn, s + 1)
                    if i >= 2:
                        act.wait_ge(s_ym, i - 1)
                        act.wait_ge(s_bv, i - 1)
                    nc.scalar.activation(nat[:, i % 2, c], ps[0][:].rearrange("p (w v) -> p w v", v=P), ACT.Copy).then_inc(s_nat, 1)

                def root_y(i):
                    act.wait_ge(s_yv, i + 1)
                    nc.scalar.activation(small[:, 48:56], small[:, 40:48], ACT.Sqrt).then_inc(s_yr, 1)

                def evac_y(i):
                    act.wait_ge(s_ytm, i + 1)
                    nc.scalar.activation(vT[:, :, i * P:(i + 1) * P], ps[7][:].rearrange("p (c t) -> p c t", t=P), ACT.Copy).then_inc(s_yt, 1)

                def square_y(i, g):
                    act.wait_ge(s_yc, i + 1)
                    if 2 * i + g:
                        act.wait_ge(s_ysr, 2 * i + g)
                    nc.scalar.activation(ysq[:], yc[:, g * 256:(g + 1) * 256], ACT.Square).then_inc(s_ysq, 1)

                nat_evac(0)
                act.wait_ge(s_xst, 16)
                def tat_evac(s):
                    i, c = divmod(s, RC)
                    act.wait_ge(s_tm, s + 1)
                    nc.scalar.activation(tat[:, i % 2, c, :], ps[3 + s % 2][:, 0:P], ACT.Copy).then_inc(s_tat, 1)

                for s in range(RC * NT):
                    i, c = divmod(s, RC)
                    act.wait_ge(s_wm, s + 1)
                    nc.scalar.activation(wv[s % 2], ps[3 + s % 2][:, 0:P], ACT.Copy).then_inc(s_we, 1)
                    act.wait_ge(s_y1m, s + 1)
                    nc.scalar.activation(y1[:, s % 2, :], ps[3 + s % 2][:, 0:256], ACT.Copy).then_inc(s_y1, 1)
                    if s:
                        tat_evac(s - 1)
                    if c == 1 and i >= 2:
                        root_y(i - 2)
                    if s + 1 < RC * NT:
                        nat_evac(s + 1)
                    if c == 2 and i >= 2:
                        evac_y(i - 2)
                    if c == 3 and i >= 1:
                        square_y(i - 1, 0)
                    if c == 0 and i >= 2:
                        square_y(i - 2, 1)
                tat_evac(RC * NT - 1)
                square_y(NT - 2, 1)
                root_y(NT - 2)
                evac_y(NT - 2)
                square_y(NT - 1, 0)
                square_y(NT - 1, 1)
                root_y(NT - 1)

                for n in range(2 * RC):
                    if n == 4:
                        evac_y(NT - 1)
                    act.wait_ge(s_gm, n + 1)
                    c, g = n // 2, n % 2
                    nc.scalar.activation(gT[:, c, g * HALF:(g + 1) * HALF], ps[n % 6][:], ACT.Copy).then_inc(s_ge, 1)
                act.wait_ge(s_or, 16)
                for c in range(RC):
                    nc.scalar.activation(oin[0][:, c, :], oraw[:, c, :], ACT.Copy).then_inc(s_wch, 1)

                def round_wo(b, loads, po):
                    act.wait_ge(s_x[0 + b], 16 + loads)
                    if po is not None:
                        act.wait_ge(s_po, po)
                    nc.scalar.activation(wo_hi[:, b], wo_raw[:, b], ACT.Copy).then_inc(s_uh, 1)

                def merged_hi(n, m0):
                    for g in range(2):
                        act.wait_ge(s_mt, m0 + (g + 1))
                        act.wait_ge(s_ctl, 6 + RC)
                        nc.scalar.activation(mg[0][:, bass.ds(n, 1), g * HALF:(g + 1) * HALF], mtmp[:, g, :], ACT.Copy).then_inc(s_mgh, 1)

                round_wo(0, 32, None)
                round_wo(1, 32, None)
                for c in range(RC):
                    act.wait_ge(s_yg, c + 1)
                    nc.scalar.activation(yin[0][:, c, :], vT[:, c, :], ACT.Copy).then_inc(s_cth, 1)
                merged_hi(0, 0)
                round_wo(0, 64, 2)
                merged_hi(1, 2)
                with act.Fori(1, KD // 2 - 1) as j:
                    round_wo(1, 32 * j + 32, 4 * j)
                    merged_hi(2 * j, 4 * j)
                    round_wo(0, 32 * j + 64, 4 * j + 2)
                    merged_hi(2 * j + 1, 4 * j + 2)
                round_wo(1, 16 * KD, 2 * (KD - 2))
                merged_hi(KD - 2, 2 * (KD - 2))
                merged_hi(KD - 1, 2 * (KD - 1))
                for k in range(KD):
                    act.wait_ge(s_x[wout_sem[k][0]], wout_sem[k][1])
                    nc.scalar.activation(wout[0][:, k, :], wout_raw[:, k % 6, :], ACT.Copy).then_inc(s_wh, 1)
                for i in range(NT):
                    act.wait_ge(s_h, 2 * i + 2)
                    if i:
                        act.wait_ge(s_ss, NT + i)
                    nc.scalar.activation(hjunk[:], hacc[:, i, :], ACT.Square, accum_out=small[:, i:i + 1]).then_inc(s_ss, 1)
                act.wait_ge(s_rt, 2 + 1)
                nc.scalar.activation(small[:, 16:24], small[:, 8:16], ACT.Sqrt).then_inc(s_rt, 1)
                for n in range(2 * KD):
                    g, k = n // KD, n % KD
                    act.wait_ge(s_tr, 2 * KD + n + 1)
                    c = VAT["norm_ffn"] + k
                    nc.scalar.activation(hT[0][:, k, g * HALF:(g + 1) * HALF], ps[n % 4][:], ACT.Copy,
                                         scale=vcol[:, c:c + 1]).then_inc(s_hi, 1)

                def round_up(b, loads, f):
                    act.wait_ge(s_x[6 + b], 16 + loads)
                    if f is not None:
                        act.wait_ge(s_f, f)
                    nc.scalar.activation(up_hi[:, b], up_raw[:, b], ACT.Copy).then_inc(s_uh, 1)

                def round_dn(b, loads, dm):
                    act.wait_ge(s_dn, loads)
                    if dm is not None:
                        act.wait_ge(s_dm, dm)
                    nc.scalar.activation(dn_hi[:, b], dn_raw[:], ACT.Copy).then_inc(s_cth, 1)

                def square(par, q, f0, dm):
                    if dm is not None:
                        act.wait_ge(s_dm, dm)
                    for h in range(2):
                        sl = slice(h * HALF, (h + 1) * HALF)
                        act.wait_ge(s_f, f0 + (2 * q + h + 1))
                        act.wait_ge(s_fl, f0 + (2 * q + h - 1) if not isinstance(f0, int) or f0 + 2 * q + h >= 1 else 0)
                        nc.scalar.activation(frelu[:, sl], ps[2 * q + h][:], ACT.Relu).then_inc(s_fr, 1)
                        act.wait_ge(s_fr, f0 + (2 * q + h + 1))
                        nc.scalar.activation(frelu[:, sl], frelu[:, sl], ACT.Square).then_inc(s_fe, 1)
                        act.wait_ge(s_fe, f0 + (2 * q + h + 1))
                        nc.scalar.activation(f_hi[:, par, q, sl], frelu[:, sl], ACT.Copy).then_inc(s_fh, 1)

                def ffn_act(g, par, first, last):
                    round_up(1, 16 * g + 16, None if first else 4 * g)
                    square(par, 0, 4 * g, None if first and par == 0 else (2 * NT * (g - 1) if not (isinstance(g, int) and g < 2) else None))
                    round_dn(par, 16 * g + 16, None if isinstance(g, int) and g < 2 else 2 * NT * (g - 1))
                    if not last:
                        round_up(0, 16 * g + 32, 4 * g + 2)
                    square(par, 1, 4 * g, None)

                round_up(0, 16, None)
                ffn_act(0, 0, True, False)
                ffn_act(1, 1, False, False)
                with act.Fori(1, NG // 2 - 1) as j:
                    ffn_act(2 * j, 0, False, False)
                    ffn_act(2 * j + 1, 1, False, False)
                ffn_act(NG - 2, 0, False, False)
                ffn_act(NG - 1, 1, False, True)
                for i in range(NT):
                    act.wait_ge(s_da, 2 * NT * (NG - 1) + 2 * i + 2)
                    act.wait_ge(s_ss, NT + NT + i)
                    nc.scalar.activation(hjunk2[:], hacc[:, i, :], ACT.Square, accum_out=small[:, 32 + i:33 + i]).then_inc(s_ss, 1)
                    act.wait_ge(s_rt, 2 + 3 + 2 * i)
                    nc.scalar.activation(small[:, 48 + i:49 + i], small[:, 40 + i:41 + i], ACT.Sqrt).then_inc(s_rt, 1)

            @block.vector
            def _(dve):
                dve_ms = nc.vector.memset(vrow[:], 0.0)
                dve_ms.then_inc(s_vec, 1)
                dve.wait_ge(s_pos, 16)
                nc.vector.tensor_copy(posr[0:NT, :], posi[0:NT, :]).then_inc(s_posf, 1)
                dve.wait_ge(s_vt, 2)
                nc.vector.tensor_copy(vcol[:, 0:NV], ps[7][:, 0:NV]).then_inc(s_vcol, 1)
                dve.wait_ge(s_const, 2)
                dch(dve, nc.vector.tensor_copy(small[:, 240:248], ps[7][:, 64:72]))
                for i in range(NT):
                    last = nc.vector.tensor_scalar(ang[:, i, :], invf[:], small[:, 240 + i:241 + i], None, ALU.mult)
                dch(dve, last)
                dch(dve, nc.vector.tensor_scalar(ang_n[:], ang[:], 1.0 / (2 * np.pi), ROUND_MAGIC, ALU.mult, ALU.add))
                dch(dve, nc.vector.tensor_scalar(ang_n[:], ang_n[:], -ROUND_MAGIC, None, ALU.add))
                for piece in TWO_PI:
                    dch(dve, nc.vector.scalar_tensor_tensor(ang[:], ang_n[:], -piece, ang[:], ALU.mult, ALU.add))
                nc.vector.tensor_scalar(ang[:], ang[:], 3.1415925, -3.1415925, ALU.min, ALU.max).then_inc(s_sin, 1)

                def inv_root(dst, root, mean_sq, t):
                    dch(dve, nc.vector.reciprocal(dst, root))
                    dch(dve, nc.vector.tensor_tensor(t, dst, dst, ALU.mult))
                    dch(dve, nc.vector.tensor_tensor(t, t, mean_sq, ALU.mult))
                    dch(dve, nc.vector.tensor_scalar(t, t, -0.5, 1.5, ALU.mult, ALU.add))
                    dch(dve, nc.vector.tensor_tensor(dst, dst, t, ALU.mult))

                def final(i):
                    dve.wait_ge(s_ss, NT + NT + i + 1)
                    nc.vector.tensor_scalar(small[:, 40 + i:41 + i], small[:, 32 + i:33 + i], 1.0 / D, NORM_EPS, ALU.mult,
                                            ALU.add).then_inc(s_rt, 1)
                    dve.wait_ge(s_rt, 2 + 4 + 2 * i)
                    inv_root(small[:, 56 + i:57 + i], small[:, 48 + i:49 + i], small[:, 40 + i:41 + i], small[:, 232:233])
                    nc.vector.scalar_tensor_tensor(hacc[:, i, :], hacc[:, i, :], small[:, 56 + i:57 + i], nfin[:], ALU.mult,
                                                   ALU.mult).then_inc(s_fin, 1)

                dve.wait_ge(s_ss, NT)
                nc.vector.tensor_scalar(small[:, 8:16], small[:, 0:8], 1.0 / D, NORM_EPS, ALU.mult,
                                        ALU.add).then_inc(s_rt, 1)
                dve.wait_ge(s_rt, 2)
                inv_root(small[:, 24:32], small[:, 16:24], small[:, 8:16], small[:, 232:240])
                for i in range(NT):
                    nc.vector.tensor_scalar(xt[:, i, :], xt[:, i, :], small[:, 24 + i:25 + i], None,
                                            ALU.mult).then_inc(s_xn, 1)
                for n in range(2 * KD):
                    g, k = n // KD, n % KD
                    c = VAT["norm_mix"] + k
                    sl = slice(g * HALF, (g + 1) * HALF)
                    dve.wait_ge(s_hi, n + 1)
                    nc.vector.scalar_tensor_tensor(uT[1][:, k, sl], ps[n % 4][:], vcol[:, c:c + 1],
                                                   uT[0][:, k, sl].bitcast(F32), ALU.mult, ALU.subtract).then_inc(s_lo, 1)
                for k in range(KD):
                    dve.wait_ge(s_wch, k + 1)
                    nc.vector.tensor_tensor(wc_lo[:, k, :], wc_raw[:, k, :], wc_hi[:, k, :].bitcast(F32),
                                            ALU.subtract).then_inc(s_wcl, 1)
                dve.wait_ge(s_sin, 3)
                dch(dve, nc.vector.tensor_tensor(cosv[:], cosv[:], cosv[:], ALU.mult))
                nc.vector.tensor_scalar(cosv[:], cosv[:], -2.0, 1.0, ALU.mult, ALU.add).then_inc(s_sin, 1)
                dve.wait_ge(s_css, 2 * NT)
                dch(dve, nc.vector.tensor_scalar(small[:, 48:56], small[:, 32:40], 1.0 / QL, NORM_EPS, ALU.mult, ALU.add))
                nc.vector.tensor_scalar(small[:, 56:64], small[:, 40:48], 1.0 / KVL, NORM_EPS, ALU.mult,
                                        ALU.add).then_inc(s_crt, 1)
                dve.wait_ge(s_crt, 2)
                inv_root(small[:, 80:96], small[:, 64:80], small[:, 48:64], small[:, 216:232])
                for i in range(NT):
                    nc.vector.tensor_scalar(cnat[:, i, 0:QL], cnat[:, i, 0:QL], small[:, 80 + i:81 + i], None, ALU.mult)
                    nc.vector.tensor_scalar(cnat[:, i, QL:QL + KVL], cnat[:, i, QL:QL + KVL], small[:, 88 + i:89 + i], None,
                                            ALU.mult).then_inc(s_cn, 1)
                for k in range(2):
                    dve.wait_ge(s_uh, k + 1)
                    nc.vector.tensor_tensor(uq_lo[:, k, :], uq_raw[:, k, :], uq_hi[:, k, :].bitcast(F32),
                                            ALU.subtract).then_inc(s_ul, 1)
                dve.wait_ge(s_uh, 3)
                nc.vector.tensor_tensor(ukv_lo[:], ukv_raw[:], ukv_hi[:].bitcast(F32), ALU.subtract).then_inc(s_ul, 1)
                for n in range(6):
                    c, g = n // 2, n % 2
                    v = (VAT["q_norm"] + c) if c < 2 else VAT["kv_norm"]
                    sl = slice(g * HALF, (g + 1) * HALF)
                    dve.wait_ge(s_cth, n + 1)
                    nc.vector.scalar_tensor_tensor(cT[1][:, c, sl], ps[n % 4][:], vcol[:, v:v + 1],
                                                   cT[0][:, c, sl].bitcast(F32), ALU.mult, ALU.subtract).then_inc(s_ctl, 1)
                for i in range(NT):
                    for b in range(2):
                        dve.wait_ge(s_qt, 4 * i + 1 + b)
                        nc.vector.tensor_copy(qT[0:QH, 4 * b:4 * b + 4, i * P:(i + 1) * P],
                                              ps[4 + b][0:QH, :].rearrange("p (h t) -> p h t", t=P)).then_inc(s_qte, 1)

                def row_max(u):
                    i = u // NH
                    dve.wait_ge(s_sc, u + 1)
                    if u == 0:
                        dve.wait_ge(s_cst2, 1)
                    if u >= 2:
                        dve.wait_ge(s_ex, ex_of(u - 2) + halves(u - 2))
                    b0, n = 2 * (u % 2), (i + 1) * P
                    db = ps[b0 + i // 4][:, (i % 4) * P:(i % 4 + 1) * P]
                    dch(dve, nc.vector.tensor_tensor(db, db, cneg[:], ALU.add))
                    m = 160 + 4 * (u % 2)
                    if n <= 512:
                        dch(dve, nc.vector.tensor_reduce(small[:, m:m + 1], ps[b0][:, 0:n], AXX, ALU.max, negate=True))
                    else:
                        dch(dve, nc.vector.tensor_reduce(small[:, m + 1:m + 2], ps[b0][:], AXX, ALU.max, negate=True))
                        dch(dve, nc.vector.tensor_reduce(small[:, m + 2:m + 3], ps[b0 + 1][:, 0:n - 512], AXX, ALU.max, negate=True))
                        dch(dve, nc.vector.tensor_tensor(small[:, m:m + 1], small[:, m + 1:m + 2], small[:, m + 2:m + 3], ALU.min))
                    nc.vector.tensor_scalar(small[:, 192 + u % 2:193 + u % 2], small[:, m:m + 1], SM_SCALE, None,
                                            ALU.mult).then_inc(s_mx, 1)

                def pt_first(u):
                    i = u // NH
                    n = min(i + 1, 4)
                    dve.wait_ge(s_pt, pt_of(u) + 1)
                    if u >= 2:
                        dve.wait_ge(s_pv, u - 1)
                    nc.vector.tensor_copy(pT[:, u % 2, 0:n, :], ps[4][:, 0:n * P].rearrange("p (b q) -> p b q", q=P)).then_inc(s_pe0, 1)

                def o_norm(i):
                    dve.wait_ge(s_pv, NH * (i + 1))
                    if i >= 2:
                        dve.wait_ge(s_ot, i - 1)
                    b = 128 + 16 * (i % 2)
                    sums = small[:, b:b + 16].rearrange("p (h two) -> p h two", two=2)
                    if i >= 4:
                        dch(dve, nc.vector.tensor_tensor(small[:, 208:216].unsqueeze(2), sums[:, :, 0:1], sums[:, :, 1:2], ALU.add))
                        dch(dve, nc.vector.reciprocal(small[:, 208:216], small[:, 208:216]))
                    else:
                        dch(dve, nc.vector.reciprocal(small[:, 208:216].unsqueeze(2), sums[:, :, 0:1]))
                    nc.vector.tensor_tensor(onat[:, i % 2, :].rearrange("p (h c) -> p h c", c=VD),
                                            ps[5 + i % 2][:].rearrange("p (h c) -> p h c", c=VD),
                                            small[:, 208:216].unsqueeze(2).to_broadcast([P, NH, VD]), ALU.mult).then_inc(s_on, 1)

                def o_evac(i):
                    dve.wait_ge(s_ot, i + 1)
                    nc.vector.tensor_copy(oT[:, :, i * P:(i + 1) * P], ps[5 + i % 2][:].rearrange("p (c t) -> p c t", t=P)).then_inc(s_ote, 1)

                for u in range(NT * NH):
                    row_max(u)
                    if u >= 1:
                        pt_first(u - 1)
                    if u % NH == 2 and u > NH:
                        o_norm(u // NH - 1)
                    if u % NH == 4 and u > NH:
                        o_evac(u // NH - 1)
                pt_first(NT * NH - 1)
                o_norm(NT - 1)
                o_evac(NT - 1)

                def rest_w(slot, wh):
                    dve.wait_ge(s_wh, wh)
                    nc.vector.tensor_tensor(w_lo[:, slot], w_raw[:, slot], w_hi[:, slot].bitcast(F32),
                                            ALU.subtract).then_inc(s_wl, 1)

                def shift(n, slot, ze):
                    dve.wait_ge(s_ze, ze)
                    dch(dve, nc.vector.tensor_tensor(zdif[:], zbuf[:, slot, 0:T], zbuf[:, slot, 1:T + 1], ALU.subtract))
                    nc.vector.scalar_tensor_tensor(z[:, n, :] if isinstance(n, int) else z[:, bass.ds(n, 1), :].squeeze(1), zdif[:],
                                                   vcol[:, bass.ds(n + VAT["mu"], 1)],
                                                   zbuf[:, slot, 1:T + 1], ALU.mult, ALU.add).then_inc(s_sh, 1)
                    dve.wait_ge(s_sh, n + 1)

                rest_w(0, 1)
                rest_w(1, 2)
                dve.wait_ge(s_z0, 1)
                dve.wait_ge(s_spo, 16)
                shift(0, 0, 2)
                rest_w(0, 3)
                shift(1, 1, 4)
                with dve.Fori(1, NRC // 2) as j:
                    dch.enter(j - 1, 2)
                    rest_w(1, 2 * j + 2)
                    shift(2 * j, 0, 4 * j + 2)
                    rest_w(0, 2 * j + 3)
                    shift(2 * j + 1, 1, 4 * j + 4)
                dch.leave(NRC // 2 - 1)
                rest_w(1, G0 + 1)
                shift(NRC - 1, 0, 2 * NRC)

                dve.wait_ge(s_z0, 2)
                def elementwise(c, last):
                    col = lambda name: vcol[:, bass.ds(c + VAT[name], 1)]
                    zr = z[:, bass.ds(c, 1), :].squeeze(1)
                    zk = z[:, bass.ds(c + RC, 1), :].squeeze(1)
                    bTc, aTc = bT[:, bass.ds(c, 1), :].squeeze(1), aT[:, bass.ds(c, 1), :].squeeze(1)
                    v3 = lambda x: x.rearrange("p (n t) -> p n t", t=CH)
                    rest_w((G0 + 1) % 2, 4 * c + (G0 + 2))
                    dve.wait_ge(s_sg, 4 * c + 2)
                    for n in range(NC):
                        ins = nc.vector.tensor_tensor_scan(cum[:, n * CH:(n + 1) * CH], kk[:, n * CH:(n + 1) * CH],
                                                           kk[:, n * CH:(n + 1) * CH], 0.0, ALU.add, ALU.max)
                    ins.then_inc(s_cum, 1)
                    dve.wait_ge(s_cum, c + 1)
                    rest_w((G0 + 2) % 2, 4 * c + (G0 + 3))
                    dch(dve, nc.vector.tensor_scalar(kk[:], zk, col("k_k"), None, ALU.mult))
                    for g in range(2):
                        dve.wait_ge(s_sq2, 2 * c + (g + 1))
                        nc.vector.tensor_scalar(rn[:, g * HALF:(g + 1) * HALF], ps[4 + g][:], 1e-24, None,
                                                ALU.max).then_inc(s_rc, 1)
                    dve.wait_ge(s_rr, c + 1)
                    dch(dve, nc.vector.reciprocal(rn[:], rn[:]))
                    rest_w((G0 + 3) % 2, 4 * c + (G0 + 4))
                    dch(dve, nc.vector.tensor_tensor(kk[:], kk[:], rn[:], ALU.mult))
                    dve.wait_ge(s_e, 3 * c + 3)
                    nc.vector.scalar_tensor_tensor(v3(aTc), v3(kk[:]), -1.0, edec[:, :, 0:CH], ALU.mult, ALU.mult)
                    dch(dve, nc.vector.tensor_tensor(bTc, kk[:], iclr[:], ALU.mult))
                    dch(dve, nc.vector.tensor_scalar(iclr[:], iclr[:], -1.0, col("k_a"), ALU.add, ALU.mult))
                    nc.vector.tensor_tensor(bTc, bTc, einv[:], ALU.mult)
                    dch(dve, nc.vector.scalar_tensor_tensor(zk, iclr[:], 1.0, zk, ALU.add, ALU.mult))
                    nc.vector.scalar_tensor_tensor(kk[:], zr, col("r_k"), zk, ALU.mult, ALU.mult).then_inc(s_rk, 1)
                    dve.wait_ge(s_rk, c + 1)
                    if not last:
                        rest_w((G0 + 4) % 2, 4 * c + (G0 + 5))
                    nc.vector.tensor_tensor(v3(zr), v3(zr), edec[:, :, 1:CH + 1], ALU.mult)
                    dch(dve, nc.vector.tensor_tensor(zk, zk, einv[:], ALU.mult))
                    dve.wait_ge(s_bs, c + 1)
                    nc.vector.tensor_copy(sbon[:, :, bass.ds(c, 1), :].squeeze(2),
                                          ps[6][:, 0:2 * NT].rearrange("p (i h) -> p i h", h=2)).then_inc(s_ew, 1)

                with dve.Fori(0, RC - 1) as c:
                    dch.enter(c, 7)
                    elementwise(c, False)
                dch.leave(RC - 1)
                elementwise(RC - 1, True)

                for n in range(2 * NT):
                    dve.wait_ge(s_lm, n + 1)
                    for r in (64, 96):
                        ins = nc.vector.tensor_copy(lc[r:r + 32, n // 2, n % 2:NH:2, :],
                                                    ps[n % 2][r:r + 32, :].rearrange("p (h s) -> p h s", s=P)[:, :, r:r + 32])
                    ins.then_inc(s_led, 1)
                dve.wait_ge(s_lp, 16)
                dve.wait_ge(s_x0, 1)
                for r in range(BL - 1):
                    cols, rows = r + 1, BL - 1 - r
                    shape = [P, 2, cols, rows]
                    prod = xprod[:, :, 0:cols * rows].rearrange("p b (s t) -> p b s t", t=rows)
                    later = xs[:, :, 0:cols, r + 1:BL]
                    dch(dve, nc.vector.tensor_tensor(prod, lp[:, :, r + 1:BL, r].unsqueeze(2).to_broadcast(shape),
                                                     xs[:, :, 0:cols, r:r + 1].to_broadcast(shape), ALU.mult))
                    ins = nc.vector.tensor_tensor(later, later, prod, ALU.add)
                    if r < BL - 2:
                        dch(dve, ins)
                ins.then_inc(s_xd, 1)

                def mask(s, h):
                    i, c = divmod(s, RC)
                    dve.wait_ge(s_pr[h], s + 1)
                    if i >= 2:
                        dve.wait_ge(s_ym, i - 1)
                    nc.vector.tensor_tensor(mq[h][:, i % 2, c, :], ps[1 + h][:], cmask[:].rearrange("p a b -> p (a b)"),
                                            ALU.mult).then_inc(s_m[h], 1)

                def u_add(n):
                    i, r = n // 2, CH * (n % 2)
                    dve.wait_ge(s_um, n + 1)
                    if i >= 2:
                        dve.wait_ge(s_ym, i - 1)
                    nc.vector.tensor_tensor(usb[r:r + CH, i % 2, :].rearrange("p (c v) -> p c v", v=P),
                                            ps[5][r:r + CH, :].rearrange("p (c v) -> p c v", v=P),
                                            taw[r:r + CH, i % 2, :, P:2 * P], ALU.add).then_inc(s_us, 1)

                def state_update(n):
                    dve.wait_ge(s_sm, n + 1)
                    if n >= 3:
                        dve.wait_ge(s_ym, (n - 3) // 2 + 1)
                    for h in range(2):
                        r = slice(64 * h, 64 * h + 64)
                        ins = nc.vector.tensor_tensor(stmp[r], ps[6][r, 0:256].rearrange("p (c v) -> p c v", v=RH),
                                                      state[r, n % 4, :, r], ALU.add)
                    dch(dve, ins)
                    for h in range(2):
                        r = slice(64 * h, 64 * h + 64)
                        ins = nc.vector.tensor_tensor(state[r, (n + 1) % 4, :, r], stmp[r],
                                                      lam[r, :, n:n + 1].to_broadcast([64, RC, RH]), ALU.mult)
                    ins.then_inc(s_st, 1)

                def y_center(i):
                    dve.wait_ge(s_ym, i + 1)
                    y3 = ps[7][:].rearrange("p (h v) -> p h v", v=RH)
                    dch(dve, nc.vector.tensor_reduce(small[:, 32:40], y3, AXX, ALU.add))
                    dch(dve, nc.vector.tensor_scalar(small[:, 32:40], small[:, 32:40], 1.0 / RH, None, ALU.mult))
                    if i:
                        dve.wait_ge(s_ytm, i)
                    nc.vector.tensor_tensor(yc[:].rearrange("p (h v) -> p h v", v=RH), y3,
                                            small[:, 32:40].unsqueeze(2).to_broadcast([P, NH, RH]), ALU.subtract).then_inc(s_yc, 1)

                def y_squares(i, g):
                    dve.wait_ge(s_ysq, 2 * i + g + 1)
                    nc.vector.tensor_reduce(small[:, 56 + 4 * g:60 + 4 * g], ysq[:].rearrange("p (h v) -> p h v", v=RH),
                                            AXX, ALU.add).then_inc(s_ysr, 1)

                def y_var(i):
                    y_squares(i, 1)
                    dve.wait_ge(s_ysr, 2 * i + 2)
                    nc.vector.tensor_scalar(small[:, 40:48], small[:, 56:64], 1.0 / RH, GN_EPS, ALU.mult, ALU.add).then_inc(s_yv, 1)

                def y_scale(i):
                    dve.wait_ge(s_yr, i + 1)
                    inv_root(small[:, 64:72], small[:, 48:56], small[:, 40:48], small[:, 72:80])
                    nc.vector.tensor_tensor(yc[:].rearrange("p (h v) -> p h v", v=RH), yc[:].rearrange("p (h v) -> p h v", v=RH),
                                            small[:, 64:72].unsqueeze(2).to_broadcast([P, NH, RH]), ALU.mult).then_inc(s_yn, 1)

                dve.wait_ge(s_msk, 1)
                dve.wait_ge(s_gs[0], 16 * GC // 2)
                dve.wait_ge(s_gs[1], 16 * GC // 2)
                mask(0, 0)
                mask(0, 1)
                def solved(s):
                    i, c = divmod(s, RC)
                    dve.wait_ge(s_y2m, s + 1)
                    nc.vector.tensor_tensor(taw[:, i % 2, c, :], ps[3 + s % 2][:, 0:256], y1[:, s % 2, :],
                                            ALU.add).then_inc(s_y2, 1)

                for s in range(RC * NT):
                    i, c = divmod(s, RC)
                    if s + 1 < RC * NT:
                        mask(s + 1, 0)
                    if s:
                        solved(s - 1)
                    if i >= 1 and c in (1, 2):
                        state_update(2 * (i - 1) + c - 1)
                    if c == 0 and i >= 2:
                        y_squares(i - 2, 0)
                    if s + 1 < RC * NT:
                        mask(s + 1, 1)
                    dve.wait_ge(s_q2m, s + 1)
                    nc.vector.tensor_copy(q2[s % 2], ps[3 + s % 2][:, 0:256]).then_inc(s_q2, 1)
                    if i >= 1 and c < 2:
                        u_add(2 * (i - 1) + c)
                    if c == 0 and i >= 2:
                        y_var(i - 2)
                    if c == 1 and i >= 2:
                        y_scale(i - 2)
                    if c == 3 and i >= 1:
                        y_center(i - 1)
                solved(RC * NT - 1)
                u_add(NC - 2)
                y_squares(NT - 2, 0)
                y_var(NT - 2)
                state_update(NC - 2)
                y_scale(NT - 2)
                u_add(NC - 1)
                y_center(NT - 1)
                y_squares(NT - 1, 0)
                y_var(NT - 1)
                y_scale(NT - 1)

                dve.wait_ge(s_yt, NT)
                for c in range(RC):
                    dve.wait_ge(s_ge, 2 * c + 2)
                    nc.vector.tensor_tensor(vT[:, c, :], vT[:, c, :], gT[:, c, :], ALU.mult).then_inc(s_yg, 1)
                for c in range(RC):
                    dve.wait_ge(s_wch, KD + c + 1)
                    nc.vector.tensor_tensor(oin[1][:, c, :], oraw[:, c, :], oin[0][:, c, :].bitcast(F32), ALU.subtract).then_inc(s_wcl, 1)

                def rest_wo(b, woh):
                    dve.wait_ge(s_uh, 3 + woh)
                    nc.vector.tensor_tensor(wo_lo[:, b], wo_raw[:, b], wo_hi[:, b].bitcast(F32), ALU.subtract).then_inc(s_ul, 1)

                def merge(n, b, loads, m0, lo_prev):
                    for g in range(2):
                        sl = slice(g * HALF, (g + 1) * HALF)
                        dve.wait_ge(s_po, m0 + (g + 1))
                        if g == 0:
                            dve.wait_ge(s_x[2 + b], 16 + loads)
                        banks = 4 * b + 2 * g
                        dch(dve, nc.vector.tensor_tensor(mtmp[:, g, :], ps[banks][:], sgate[:, b, 0, sl], ALU.mult))
                        dch(dve, nc.vector.tensor_tensor(sgate[:, b, 1, sl], ps[banks + 1][:], sgate[:, b, 1, sl], ALU.mult))
                        nc.vector.tensor_tensor(mtmp[:, g, :], mtmp[:, g, :], sgate[:, b, 1, sl], ALU.add).then_inc(s_mt, 1)
                        dve.wait_ge(s_mt, m0 + (g + 1))
                        dve.wait_ge(s_mgh, m0 + (g + 1))
                        nc.vector.tensor_tensor(mg[1][:, bass.ds(n, 1), sl].squeeze(1), mtmp[:, g, :],
                                                mg[0][:, bass.ds(n, 1), sl].squeeze(1).bitcast(F32), ALU.subtract).then_inc(s_mgl, 1)

                rest_wo(0, 1)
                rest_wo(1, 2)
                for c in range(RC):
                    dve.wait_ge(s_cth, 6 + c + 1)
                    nc.vector.tensor_tensor(yin[1][:, c, :], vT[:, c, :], yin[0][:, c, :].bitcast(F32), ALU.subtract).then_inc(s_ctl, 1)
                merge(0, 0, 32, 0, None)
                rest_wo(0, 3)
                merge(1, 1, 32, 2, None)
                with dve.Fori(1, KD // 2 - 1) as j:
                    dch.enter(j - 1, 8)
                    rest_wo(1, 2 * j + 2)
                    merge(2 * j, 0, 32 * j + 32, 4 * j, None)
                    rest_wo(0, 2 * j + 3)
                    merge(2 * j + 1, 1, 32 * j + 32, 4 * j + 2, None)
                dch.leave(KD // 2 - 2)
                rest_wo(1, KD)
                merge(KD - 2, 0, 16 * KD, 2 * (KD - 2), None)
                merge(KD - 1, 1, 16 * KD, 2 * (KD - 1), None)
                for k in range(KD):
                    dve.wait_ge(s_wh, (G0 + GC) + k + 1)
                    nc.vector.tensor_tensor(wout[1][:, k, :], wout_raw[:, k % 6, :], wout[0][:, k, :].bitcast(F32),
                                            ALU.subtract).then_inc(s_wl, 1)
                dve.wait_ge(s_hx, 16 * NT)
                for n in range(2 * NT):
                    sl = slice((n % 2) * HALF, (n % 2 + 1) * HALF)
                    dve.wait_ge(s_hm, n + 1)
                    nc.vector.tensor_tensor(hacc[:, n // 2, sl], hacc[:, n // 2, sl], ps[n % 4][:], ALU.add).then_inc(s_h, 1)
                dve.wait_ge(s_ss, NT + NT)
                nc.vector.tensor_scalar(small[:, 8:16], small[:, 0:8], 1.0 / D, NORM_EPS, ALU.mult, ALU.add).then_inc(s_rt, 1)
                dve.wait_ge(s_rt, 2 + 2)
                inv_root(small[:, 24:32], small[:, 16:24], small[:, 8:16], small[:, 232:240])
                for i in range(NT):
                    nc.vector.tensor_scalar(hn[:, i, :], hacc[:, i, :], small[:, 24 + i:25 + i], None, ALU.mult).then_inc(s_xn, 1)
                for n in range(2 * KD):
                    g, k = n // KD, n % KD
                    c = VAT["norm_ffn"] + k
                    sl = slice(g * HALF, (g + 1) * HALF)
                    dve.wait_ge(s_hi, 2 * KD + n + 1)
                    nc.vector.scalar_tensor_tensor(hT[1][:, k, sl], ps[n % 4][:], vcol[:, c:c + 1],
                                                   hT[0][:, k, sl].bitcast(F32), ALU.mult, ALU.subtract).then_inc(s_lo, 1)

                def rest_up(b, uph):
                    dve.wait_ge(s_uh, (3 + KD) + uph)
                    nc.vector.tensor_tensor(up_lo[:, b], up_raw[:, b], up_hi[:, b].bitcast(F32), ALU.subtract).then_inc(s_ul, 1)

                def rest_f(par, q, f0):
                    for h in range(2):
                        sl = slice(h * HALF, (h + 1) * HALF)
                        dve.wait_ge(s_fh, f0 + (2 * q + h + 1))
                        nc.vector.tensor_tensor(f_lo[:, par, q, sl], frelu[:, sl], f_hi[:, par, q, sl].bitcast(F32),
                                                ALU.subtract).then_inc(s_fl, 1)

                def ffn_split(g, par, last):
                    rest_up(1, 2 * g + 2)
                    rest_f(par, 0, 4 * g)
                    dve.wait_ge(s_cth, (6 + RC) + g + 1)
                    nc.vector.tensor_tensor(dn_lo[:, par], dn_raw[:], dn_hi[:, par].bitcast(F32), ALU.subtract).then_inc(s_ctl, 1)
                    if not last:
                        rest_up(0, 2 * g + 3)
                    rest_f(par, 1, 4 * g)

                def down_add(d0):
                    for n in range(2 * NT):
                        sl = slice((n % 2) * HALF, (n % 2 + 1) * HALF)
                        dve.wait_ge(s_dm, d0 + (n + 1))
                        nc.vector.tensor_tensor(hacc[:, n // 2, sl], hacc[:, n // 2, sl], ps[4 + n % 4][:], ALU.add).then_inc(s_da, 1)

                rest_up(0, 1)
                ffn_split(0, 0, False)
                ffn_split(1, 1, False)
                down_add(0)
                with dve.Fori(1, NG // 2 - 1) as j:
                    ffn_split(2 * j, 0, False)
                    down_add(2 * NT * (2 * j - 1))
                    ffn_split(2 * j + 1, 1, False)
                    down_add(4 * NT * j)
                ffn_split(NG - 2, 0, False)
                down_add(2 * NT * (NG - 3))
                ffn_split(NG - 1, 1, True)
                down_add(2 * NT * (NG - 2))
                dve.wait_ge(s_nf, 16)
                for i in range(NT):
                    for h in range(2):
                        n = 2 * i + h
                        sl = slice(h * HALF, (h + 1) * HALF)
                        dve.wait_ge(s_dm, 2 * NT * (NG - 1) + n + 1)
                        nc.vector.tensor_tensor(hacc[:, i, sl], hacc[:, i, sl], ps[4 + n % 4][:], ALU.add).then_inc(s_da, 1)
                    if i:
                        final(i - 1)
                final(NT - 1)

            @block.tensor
            def _(pe):
                pe.wait_ge(s_const, 1)
                pe.wait_ge(s_vec, 1 + 16 * len(VROWS))
                nc.tensor.transpose(ps[7][:, 0:NV], vrow[0:NV, :], ident[0:NV, 0:NV]).then_inc(s_vt, 1)
                pe.wait_ge(s_posf, 1)
                nc.tensor.transpose(ps[7][:, 64:64 + NT], posr[0:NT, :], ident[0:NT, 0:NT]).then_inc(s_vt, 1)
                for n in range(2 * KD):
                    g, k = n // KD, n % KD
                    if k == 0:
                        pe.wait_ge(s_xn, 4 * (g + 1))
                    if n >= 4:
                        pe.wait_ge(s_lo, n - 3)
                    for j in range(4):
                        ins = nc.tensor.transpose(ps[n % 4][:, j * P:(j + 1) * P],
                                                  xt[:, 4 * g + j, k * P:(k + 1) * P], ident[:])
                    ins.then_inc(s_tr, 1)
                pe.wait_ge(s_lo, 2 * KD)
                for i in range(NT):
                    if i >= 2:
                        pe.wait_ge(s_ce, i - 1)
                    tok = slice(i * P, (i + 1) * P)
                    for k in range(KD):
                        if i == 0:
                            pe.wait_ge(s_wcl, k + 1)
                        for m, (st, mv) in enumerate(((uT[0], wc_hi), (uT[1], wc_hi), (uT[0], wc_lo))):
                            ins = nc.tensor.matmul(ps[4 + i % 2][:, 0:CC], st[:, k, tok], mv[:, k, :],
                                                   start=(k == 0 and m == 0), stop=(k == KD - 1 and m == 2))
                    ins.then_inc(s_cp, 1)
                pe.wait_ge(s_cn, NT)
                for n in range(6):
                    c, g = n // 2, n % 2
                    if n >= 4:
                        pe.wait_ge(s_ctl, n - 3)
                    for j in range(4):
                        ins = nc.tensor.transpose(ps[n % 4][:, j * P:(j + 1) * P],
                                                  cnat[:, 4 * g + j, c * P:(c + 1) * P], ident[:])
                    ins.then_inc(s_ct, 1)
                pe.wait_ge(s_ctl, 6)
                pe.wait_ge(s_ul, 3)

                def project(i):
                    tok = slice(i * P, (i + 1) * P)
                    if i:
                        pe.wait_ge(s_qe, 5 * i)
                    for b in range(2):
                        col = slice(b * 4 * QH, (b + 1) * 4 * QH)
                        for k in range(2):
                            for m, (st, mv) in enumerate(((cT[0], uq_hi), (cT[1], uq_hi), (cT[0], uq_lo))):
                                ins = nc.tensor.matmul(ps[b][:, 0:4 * QH], st[:, k, tok], mv[:, k, col],
                                                       start=(k == 0 and m == 0), stop=(k == 1 and m == 2))
                        ins.then_inc(s_qp, 1)
                    for b in range(2):
                        col = slice(b * 512, (b + 1) * 512)
                        for m, (st, mv) in enumerate(((cT[0], ukv_hi), (cT[1], ukv_hi), (cT[0], ukv_lo))):
                            ins = nc.tensor.matmul(ps[2 + b][:], st[:, 2, tok], mv[:, col],
                                                   start=(m == 0), stop=(m == 2))
                        ins.then_inc(s_qp, 1)

                project(0)
                for i in range(NT):
                    if i + 1 < NT:
                        project(i + 1)
                    pe.wait_ge(s_ro, i + 1)
                    for t, rows in enumerate((q_nat, k_nat)):
                        for b in range(2):
                            if i:
                                pe.wait_ge(s_qte, 4 * i)
                            for h in range(4):
                                ins = nc.tensor.transpose(ps[4 + 2 * t + b][0:QH, h * P:(h + 1) * P],
                                                          rows[:, 4 * b + h, :], ident[:])
                            ins.then_inc(s_qt, 1)

                def scores(u):
                    i, h = u // NH, u % NH
                    n, b0 = (i + 1) * P, 2 * (u % 2)
                    if u >= 2:
                        pe.wait_ge(s_ex, ex_of(u - 2) + halves(u - 2))
                    for g in range(halves(u)):
                        w = min(n - 512 * g, 512)
                        ins = nc.tensor.matmul(ps[b0 + g][:, 0:w], qT[0:QH, h, i * P:(i + 1) * P],
                                               kT[0:QH, h, 512 * g:512 * g + w], start=True, stop=True)
                    ins.then_inc(s_sc, 1)

                def transpose_probs(u):
                    i = u // NH
                    for g in range(groups(u)):
                        pe.wait_ge(s_ex, ex_of(u) + g + 1)
                        if g == 0 and u >= 1:
                            pe.wait_ge(s_pe0, u)
                        if g == 1 and second_of(u):
                            pe.wait_ge(s_pe1, second_of(u))
                        for b in range(4 * g, min(i + 1, 4 * g + 4)):
                            ins = nc.tensor.transpose(ps[4 if g == 0 else 7][:, (b % 4) * P:(b % 4 + 1) * P],
                                                      pexp[:, u % 2, b * P:(b + 1) * P], ident[:])
                        ins.then_inc(s_pt, 1)

                def values(u):
                    i, h = u // NH, u % NH
                    pe.wait_ge(s_pe0, u + 1)
                    if groups(u) == 2:
                        pe.wait_ge(s_pe1, second_of(u) + 1)
                    if h == 0 and i >= 2:
                        pe.wait_ge(s_ote, i - 1)
                    for b in range(i + 1):
                        ins = nc.tensor.matmul(ps[5 + i % 2][:, h * VD:(h + 1) * VD], pT[:, u % 2, b, :],
                                               vm[:, b, h * VD:(h + 1) * VD], start=(b == 0), stop=(b == i))
                    ins.then_inc(s_pv, 1)

                def transpose_o(i):
                    pe.wait_ge(s_on, i + 1)
                    for c in range(4):
                        ins = nc.tensor.transpose(ps[5 + i % 2][:, c * P:(c + 1) * P], onat[:, i % 2, c * P:(c + 1) * P], ident[:])
                    ins.then_inc(s_ot, 1)

                pe.wait_ge(s_qte, 4 * NT)
                scores(0)
                for u in range(NT * NH):
                    if u + 1 < NT * NH:
                        scores(u + 1)
                    if u >= 1:
                        values(u - 1)
                    transpose_probs(u)
                    if u % NH == 3 and u > NH:
                        transpose_o(u // NH - 1)
                values(NT * NH - 1)
                transpose_o(NT - 1)

                def chunk(slot, wl, ze, pools=()):
                    pe.wait_ge(s_wl, wl)
                    for g in range(2):
                        if ze is not None:
                            pe.wait_ge(s_ze, ze + (g + 1))
                        for k in range(KD):
                            for m, (st, mv) in enumerate(((w_hi, uT[0]), (w_lo, uT[0]), (w_hi, uT[1]))):
                                ins = nc.tensor.matmul(ps[2 * slot + g][:], st[:, slot, k, :], mv[:, k, g * HALF:(g + 1) * HALF],
                                                       start=(k == 0 and m == 0), stop=(k == KD - 1 and m == 2))
                        ins.then_inc(s_pj, 1)

                chunk(0, 1, None)
                chunk(1, 2, None)
                with pe.Fori(1, NRC // 2) as j:
                    chunk(0, 2 * j + 1, 4 * j - 4)
                    chunk(1, 2 * j + 2, 4 * j - 2)
                chunk(0, NRC, 2 * (NRC - 3))
                pe.wait_ge(s_bo, 3)
                pe.wait_ge(s_zs, 1)

                def gates_and_rwkv(c):
                    def gate(q):
                        n = G0 + q
                        chunk(n % 2, 4 * c + (n + 1), 8 * c + 2 * (n - 2))

                    gate(0)
                    pe.wait_ge(s_wau, 32 * c + 32)
                    if not isinstance(c, int):
                        pe.wait_ge(s_ew, c)
                    for r, b0 in ((0, 4), (64, 6)):
                        for g in range(2):
                            nc.tensor.matmul(ps[b0 + g][:], wau[r:r + 64, :], z[r:r + 64, 3 * RC, g * HALF:(g + 1) * HALF],
                                             start=True, stop=True).then_inc(s_pre, 1)
                    gate(1)
                    pe.wait_ge(s_sq, c + 1)
                    for g in range(2):
                        nc.tensor.matmul(ps[4 + g][:], bones[:], rn[:, g * HALF:(g + 1) * HALF],
                                         start=True, stop=True).then_inc(s_sq2, 1)
                    gate(2)
                    gate(3)
                    pe.wait_ge(s_rk, c + 1)
                    for i in range(NT):
                        ins = nc.tensor.matmul(ps[6][:, 2 * i:2 * i + 2], kk[:, i * P:(i + 1) * P], bones[:, 0:P:64],
                                               start=True, stop=True)
                    ins.then_inc(s_bs, 1)

                gates_and_rwkv(0)
                with pe.Fori(1, RC) as c:
                    gates_and_rwkv(c)

                pe.wait_ge(s_ew, RC)
                pe.wait_ge(s_ze, 2 * (G0 + GC))
                for n in range(2 * NT):
                    i = n // 2
                    if n >= 2:
                        pe.wait_ge(s_lea, n - 1)
                        pe.wait_ge(s_led, n - 1)
                    r = 64 * (n % 2)
                    for c in range(RC):
                        ins = nc.tensor.matmul(ps[n % 2][:, c * P:(c + 1) * P], aT[r:r + 64, c, i * P:(i + 1) * P],
                                               bT[r:r + 64, c, i * P:(i + 1) * P], start=True, stop=True)
                    ins.then_inc(s_lm, 1)

                def naturals(s):
                    i, c = divmod(s, RC)
                    tok = slice(i * P, (i + 1) * P)
                    if s:
                        pe.wait_ge(s_nat, s)
                    for w, src in enumerate((aT[:, c, tok], bT[:, c, tok], z[:, RC + c, tok], vT[:, c, tok])):
                        ins = nc.tensor.transpose(ps[0][:, w * P:(w + 1) * P], src, ident[:])
                    ins.then_inc(s_tn, 1)

                def products(s, h):
                    i, c = divmod(s, RC)
                    tok, r = slice(i * P, (i + 1) * P), 64 * h
                    if s:
                        pe.wait_ge(s_m[h], s)
                    for w, st in enumerate((bT[r:r + 64, c, tok], z[r:r + 64, RC + c, tok])):
                        for v, mv_ in enumerate((aT[r:r + 64, c, tok], z[r:r + 64, c, tok])):
                            at = (2 * w + v) * P
                            ins = nc.tensor.matmul(ps[1 + h][:, at:at + P], st, mv_, start=True, stop=True)
                    ins.then_inc(s_pr[h], 1)

                def view(x, h):
                    return x.rearrange("p (w h v) -> p w h v", w=2, h=2)[:, :, h, :]

                def part(s):
                    return ps[3 + s % 2][:, 0:256]

                def mv(s):
                    i, c = divmod(s, RC)
                    pe.wait_ge(s_nat, s + 1)
                    pe.wait_ge(s_m[0], s + 1)
                    pe.wait_ge(s_m[1], s + 1)
                    if s >= 2:
                        pe.wait_ge(s_tat, s - 1)
                    for h in range(2):
                        ins = nc.tensor.matmul(part(s)[:, h * RH:(h + 1) * RH], mq[h][:, i % 2, c, 2 * P:3 * P],
                                               nat[:, i % 2, c, 3, h * RH:(h + 1) * RH], start=True, stop=True)
                    ins.then_inc(s_wm, 1)

                def block_solve(s):
                    i, c = divmod(s, RC)
                    pe.wait_ge(s_we, s + 1)
                    for h in range(2):
                        st = zz[:, NH * i + 2 * c + h, :]
                        nc.tensor.matmul(part(s)[:, h * RH:(h + 1) * RH], st, nat[:, i % 2, c, 0, h * RH:(h + 1) * RH],
                                         start=True, stop=True)
                        ins = nc.tensor.matmul(part(s)[:, P + h * RH:P + (h + 1) * RH], st, wv[s % 2][:, h * RH:(h + 1) * RH],
                                               start=True, stop=True)
                    ins.then_inc(s_y1m, 1)

                def offblock(s):
                    i, c = divmod(s, RC)
                    pe.wait_ge(s_y1, s + 1)
                    for h in range(2):
                        ins = nc.tensor.matmul(view(part(s), h), mq[h][:, i % 2, c, 0:P], view(y1[:, s % 2, :], h),
                                               start=True, stop=True)
                    ins.then_inc(s_q2m, 1)

                def correct(s):
                    i, c = divmod(s, RC)
                    pe.wait_ge(s_q2, s + 1)
                    for h in range(2):
                        ins = nc.tensor.matmul(view(part(s), h), zz[:, NH * i + 2 * c + h, :], view(q2[s % 2], h),
                                               start=True, stop=True)
                    ins.then_inc(s_y2m, 1)

                def transpose_ta(s):
                    i, c = divmod(s, RC)
                    pe.wait_ge(s_y2, s + 1)
                    nc.tensor.transpose(part(s)[:, 0:P], taw[:, i % 2, c, 0:P], ident[:]).then_inc(s_tm, 1)

                def u_product(n):
                    i, r = n // 2, CH * (n % 2)
                    pe.wait_ge(s_tat, RC * (i + 1))
                    pe.wait_ge(s_st, n + 1)
                    if n:
                        pe.wait_ge(s_us, n)
                    for c in range(RC):
                        ins = nc.tensor.matmul(ps[5][r:r + CH, c * P:(c + 1) * P], tat[:, i % 2, c, r:r + CH],
                                               state[:, n % 4, c, :], start=True, stop=True)
                    ins.then_inc(s_um, 1)

                def state_product(n):
                    i, r = n // 2, CH * (n % 2)
                    pe.wait_ge(s_us, n + 1)
                    for c in range(RC):
                        for h in range(2):
                            o = ps[6][64 * h:64 * h + 64, c * RH:(c + 1) * RH]
                            v0 = slice(h * RH, (h + 1) * RH)
                            nc.tensor.matmul(o, nat[r:r + CH, i % 2, c, 1, v0], usb[r:r + CH, i % 2, c * P + h * RH:c * P + (h + 1) * RH],
                                             start=True, stop=False)
                            ins = nc.tensor.matmul(o, nat[r:r + CH, i % 2, c, 2, v0], nat[r:r + CH, i % 2, c, 3, v0],
                                                   start=False, stop=True)
                    ins.then_inc(s_sm, 1)

                def y_product(i):
                    pe.wait_ge(s_us, 2 * i + 2)
                    if i:
                        pe.wait_ge(s_yt, i)
                    for c in range(RC):
                        for m in range(2):
                            r = CH * m
                            nc.tensor.matmul(ps[7][r:r + CH, c * P:(c + 1) * P], z[:, c, i * P + r:i * P + r + CH],
                                             state[:, (2 * i + m) % 4, c, :], start=True, stop=False, skip_group_check=True)
                        for h in range(2):
                            v0 = slice(h * RH, (h + 1) * RH)
                            o = slice(c * P + h * RH, c * P + (h + 1) * RH)
                            nc.tensor.matmul(ps[7][:, o], mq[h][:, i % 2, c, 3 * P:4 * P], nat[:, i % 2, c, 3, v0],
                                             start=False, stop=False, skip_group_check=True)
                            ins = nc.tensor.matmul(ps[7][:, o], mq[h][:, i % 2, c, P:2 * P], usb[:, i % 2, o],
                                                   start=False, stop=True, skip_group_check=True)
                    ins.then_inc(s_ym, 1)

                def transpose_y(i):
                    pe.wait_ge(s_pn, i + 1)
                    for c in range(RC):
                        ins = nc.tensor.transpose(ps[7][:, c * P:(c + 1) * P], yc[:, c * P:(c + 1) * P], ident[:])
                    ins.then_inc(s_ytm, 1)

                pe.wait_ge(s_v, 16)
                pe.wait_ge(s_lea, 2 * NT)
                pe.wait_ge(s_led, 2 * NT)
                naturals(0)
                products(0, 0)
                products(0, 1)
                for s in range(RC * NT):
                    i, c = divmod(s, RC)
                    more = s + 1 < RC * NT
                    mv(s)
                    if more:
                        products(s + 1, 0)
                    if c == 3 and i >= 1:
                        y_product(i - 1)
                    if s:
                        correct(s - 1)
                    if i >= 1 and c in (1, 2):
                        state_product(2 * (i - 1) + c - 1)
                    if s == 0:
                        pe.wait_ge(s_zz, 64)
                    block_solve(s)
                    if more:
                        products(s + 1, 1)
                    if s:
                        transpose_ta(s - 1)
                    if more:
                        naturals(s + 1)
                    offblock(s)
                    if c == 2 and i >= 2:
                        transpose_y(i - 2)
                    if i >= 1 and c < 2:
                        u_product(2 * (i - 1) + c)
                correct(RC * NT - 1)
                transpose_ta(RC * NT - 1)
                u_product(NC - 2)
                state_product(NC - 2)
                u_product(NC - 1)
                transpose_y(NT - 2)
                y_product(NT - 1)
                pe.wait_ge(s_gup, 48)
                for n in range(2 * RC):
                    c, sl = n // 2, slice((n % 2) * HALF, (n % 2 + 1) * HALF)
                    if n == 6:
                        transpose_y(NT - 1)
                    if n >= 6:
                        pe.wait_ge(s_ge, n - 5)
                    nc.tensor.matmul(ps[n % 6][:], gup[:, 0, c * P:(c + 1) * P], sg2[:, 0, sl], start=True, stop=False)
                    nc.tensor.matmul(ps[n % 6][:], gup[0:LORA_G - P, 1, c * P:(c + 1) * P], sg2[0:LORA_G - P, 1, sl],
                                     start=False, stop=True).then_inc(s_gm, 1)

                def branch(b, g, w):
                    src, sl = (yin, oin)[w], slice(g * HALF, (g + 1) * HALF)
                    for k in range(RC):
                        for m, (st, mv_) in enumerate(((wo_hi, src[0]), (wo_lo, src[0]), (wo_hi, src[1]))):
                            ins = nc.tensor.matmul(ps[4 * b + 2 * g + w][:], st[:, b, w, k, :], mv_[:, k, sl],
                                                   start=(k == 0 and m == 0), stop=(k == RC - 1 and m == 2))
                    return ins

                def branches(b, wol, mt):
                    pe.wait_ge(s_ul, 3 + wol)
                    for g in range(2):
                        pe.wait_ge(s_mt, mt + (g + 1))
                        branch(b, g, 1)
                        branch(b, g, 0).then_inc(s_po, 1)

                pe.wait_ge(s_wcl, KD + RC)
                pe.wait_ge(s_ge, 2 * RC)
                pe.wait_ge(s_yt, NT)
                for b in range(2):
                    pe.wait_ge(s_ul, 3 + b + 1)
                    for g in range(2):
                        branch(b, g, 1)
                pe.wait_ge(s_ctl, 6 + RC)
                for b in range(2):
                    for g in range(2):
                        branch(b, g, 0).then_inc(s_po, 1)
                with pe.Fori(1, KD // 2) as j:
                    branches(0, 2 * j + 1, 4 * j - 4)
                    branches(1, 2 * j + 2, 4 * j - 2)
                pe.wait_ge(s_mgl, 2 * KD)
                for n in range(2 * NT):
                    i, sl = n // 2, slice((n % 2) * HALF, (n % 2 + 1) * HALF)
                    if n >= 4:
                        pe.wait_ge(s_h, n - 3)
                    for k in range(KD):
                        if n == 0:
                            pe.wait_ge(s_wl, (G0 + GC) + k + 1)
                        for m, (st, mv_) in enumerate(((mg[0], wout[0]), (mg[1], wout[0]), (mg[0], wout[1]))):
                            ins = nc.tensor.matmul(ps[n % 4][:], st[:, k, i * P:(i + 1) * P], mv_[:, k, sl],
                                                   start=(k == 0 and m == 0), stop=(k == KD - 1 and m == 2))
                    ins.then_inc(s_hm, 1)
                for n in range(2 * KD):
                    g, k = n // KD, n % KD
                    if k == 0:
                        pe.wait_ge(s_xn, NT + 4 * (g + 1))
                    if n >= 4:
                        pe.wait_ge(s_lo, 2 * KD + n - 3)
                    for j in range(4):
                        ins = nc.tensor.transpose(ps[n % 4][:, j * P:(j + 1) * P], hn[:, 4 * g + j, k * P:(k + 1) * P], ident[:])
                    ins.then_inc(s_tr, 1)
                pe.wait_ge(s_lo, 2 * KD + 2 * KD)

                def up(upl, f0):
                    for q in range(2):
                        pe.wait_ge(s_ul, (3 + KD) + upl + q)
                        for h in range(2):
                            sl = slice(h * HALF, (h + 1) * HALF)
                            if f0 is not None:
                                pe.wait_ge(s_fr, f0 + (2 * q + h + 1))
                            for k in range(KD):
                                for m, (st, mv_) in enumerate(((up_hi, hT[0]), (up_lo, hT[0]), (up_hi, hT[1]))):
                                    ins = nc.tensor.matmul(ps[2 * q + h][:], st[:, q, k, :], mv_[:, k, sl],
                                                           start=(k == 0 and m == 0), stop=(k == KD - 1 and m == 2))
                            ins.then_inc(s_f, 1)

                def down(par, fl, dnl, d0):
                    pe.wait_ge(s_fl, fl)
                    pe.wait_ge(s_ctl, (6 + RC) + dnl)
                    for n in range(2 * NT):
                        i, sl = n // 2, slice((n % 2) * HALF, (n % 2 + 1) * HALF)
                        if not isinstance(d0, int) or d0 + n >= 4:
                            pe.wait_ge(s_da, d0 + (n - 3))
                        for q in range(2):
                            for m, (st, mv_) in enumerate(((f_hi, dn_hi), (f_lo, dn_hi), (f_hi, dn_lo))):
                                ins = nc.tensor.matmul(ps[4 + n % 4][:], st[:, par, q, i * P:(i + 1) * P], mv_[:, par, q, sl],
                                                       start=(q == 0 and m == 0), stop=(q == 1 and m == 2))
                        ins.then_inc(s_dm, 1)

                up(1, None)
                up(3, 0)
                down(0, 4, 1, 0)
                with pe.Fori(1, NG // 2) as j:
                    up(4 * j + 1, 8 * j - 4)
                    down(1, 8 * j, 2 * j, 2 * NT * (2 * j - 1))
                    up(4 * j + 3, 8 * j)
                    down(0, 8 * j + 4, 2 * j + 1, 4 * NT * j)
                down(1, 4 * NG, NG, 2 * NT * (NG - 1))


_INS = ['x', 'positions', 'norm_mix', 'w_in', 'mu_shift', 'w0', 'w_up', 'a0', 'a_up', 'g_up', 'k_k', 'k_a', 'r_k', 'ln_w',
        'ln_b', 'w_o_rwkv', 'q_norm', 'w_uq', 'kv_norm', 'w_ukv', 'w_o_mla', 'w_out', 'norm_ffn', 'w_ff_up', 'w_ff_down',
        'norm_final']


def kernel(**inputs):
    import concourse.bacc as bacc
    from concourse.bass_utils import run_bass_kernel_spmd

    nc = bacc.Bacc("TRN2", target_bir_lowering=False, num_devices=1)
    arrays, aps = {}, {}
    for name in _INS:
        v = np.ascontiguousarray(inputs[name])
        arrays[f"in_{name}"] = v
        aps[name] = nc.dram_tensor(f"in_{name}", v.shape, mybir.dt.from_np(v.dtype), kind="ExternalInput").ap()
    out = nc.dram_tensor("out_0", (1, T, D), F32, kind="ExternalOutput").ap()
    program(nc, aps, out)
    r = run_bass_kernel_spmd(nc, [arrays], core_ids=[0])
    return r.results[0]["out_0"]
```
